# Optimizing a Trainium2 kernel written in Bass

```python
import jax, jax.numpy as jnp
from jax import lax
import numpy as np

D_MODEL = 2048
BATCH = 1
SEQ = 256
DEPTH = 1

MEM_LEN = 256
CHUNK = 64
EPS = 1e-6
GLA_HEADS = 4
GLA_DK = D_MODEL // 16
GLA_DV = D_MODEL // 8
GLA_QK = GLA_HEADS * GLA_DK
GLA_V = GLA_HEADS * GLA_DV
GLA_RANK = 16
GLA_TAU = 16.0
GDN_HEADS = 8
GDN_DK = D_MODEL // 16
GDN_DV = D_MODEL // 16
GDN_QK = GDN_HEADS * GDN_DK
GDN_V = GDN_HEADS * GDN_DV
CONV_W = 4
XA_HEADS = 4
XA_DH = D_MODEL // 8
XA_W = XA_HEADS * XA_DH
N_BRANCH = 3
D_FF = ((8 * D_MODEL // 3 + 255) // 256) * 256
IN_SIZES = (GLA_QK, GLA_QK, GLA_V, GLA_RANK, GLA_V,
            2 * GDN_QK + GDN_V, GDN_HEADS, GDN_HEADS, GDN_V,
            XA_W, N_BRANCH * D_MODEL)
W_IN_COLS = sum(IN_SIZES)

kernel_name = "hybrid_gla_gdn_memxattn_macaron"

def rmsnorm(x, w):
    xf = x.astype(jnp.float32)
    y = xf * lax.rsqrt(jnp.mean(xf * xf, axis=-1, keepdims=True) + EPS)
    return (y * w.astype(jnp.float32)).astype(x.dtype)

def l2norm(x):
    return x * lax.rsqrt(jnp.sum(x * x, axis=-1, keepdims=True) + EPS)

def swiglu(x, w_gu, w_down):
    g, u = jnp.split(x @ w_gu, 2, axis=-1)
    return (jax.nn.silu(g) * u) @ w_down

def to_chunks(t):
    b, s, h, d = t.shape
    return t.reshape(b, s // CHUNK, CHUNK, h, d).transpose(1, 0, 3, 2, 4)

def from_chunks(t):
    n, b, h, c, d = t.shape
    return t.transpose(1, 0, 3, 2, 4).reshape(b, n * c, h, d)

def heads_to_chunks(t):
    b, s, h = t.shape
    return t.reshape(b, s // CHUNK, CHUNK, h).transpose(1, 0, 3, 2)

def causal_short_conv(x, w):
    ch = x.shape[-1]
    y = lax.conv_general_dilated(x, w[:, None, :].astype(x.dtype), window_strides=(1,),
                                 padding=[(CONV_W - 1, 0)],
                                 dimension_numbers=('NWC', 'WIO', 'NWC'),
                                 feature_group_count=ch)
    return jax.nn.silu(y)

def gla_chunked(q, k, v, logg):
    b, s, h, dk = q.shape
    dv = v.shape[-1]
    causal = jnp.tril(jnp.ones((CHUNK, CHUNK), dtype=bool))

    def step(state, inp):
        q_, k_, v_, g_ = inp
        cb = jnp.cumsum(g_, axis=2)
        o_inter = jnp.einsum('bhcd,bhde->bhce', q_ * jnp.exp(cb), state)
        diff = cb[:, :, :, None, :] - cb[:, :, None, :, :]
        dec = jnp.exp(jnp.where(causal[:, :, None], diff, -jnp.inf))
        attn = jnp.einsum('bhid,bhjd,bhijd->bhij', q_, k_, dec)
        o = o_inter + jnp.einsum('bhij,bhje->bhie', attn, v_)
        c_last = cb[:, :, -1:, :]
        state = (jnp.exp(c_last[:, :, 0, :])[..., None] * state
                 + jnp.einsum('bhcd,bhce->bhde', k_ * jnp.exp(c_last - cb), v_))
        return state, o

    init = jnp.zeros((b, h, dk, dv), jnp.float32)
    _, o = lax.scan(step, init, (to_chunks(q), to_chunks(k), to_chunks(v), to_chunks(logg)))
    return from_chunks(o)

def gdn_chunked(q, k, v, g, beta):
    b, s, h, dk = q.shape
    dv = v.shape[-1]
    qc, kc, vc = to_chunks(q), to_chunks(k), to_chunks(v)
    gcum = jnp.cumsum(heads_to_chunks(g), axis=-1)
    bc = heads_to_chunks(beta)[..., None]
    causal = jnp.tril(jnp.ones((CHUNK, CHUNK), dtype=bool))
    strict = jnp.tril(jnp.ones((CHUNK, CHUNK), dtype=bool), -1)
    diff = gcum[..., :, None] - gcum[..., None, :]
    decay = jnp.where(causal, jnp.exp(jnp.where(causal, diff, 0.0)), 0.0)
    k_beta = kc * bc
    lower = jnp.where(strict, jnp.einsum('nbhid,nbhjd->nbhij', k_beta, kc) * decay, 0.0)
    tmat = lower + jnp.eye(CHUNK, dtype=lower.dtype)
    u = lax.linalg.triangular_solve(tmat, vc * bc, left_side=True, lower=True, unit_diagonal=True)
    w = lax.linalg.triangular_solve(tmat, k_beta * jnp.exp(gcum)[..., None],
                                    left_side=True, lower=True, unit_diagonal=True)

    def step(state, inp):
        q_, k_, u_, w_, gc_, dec_ = inp
        attn = jnp.where(causal, jnp.einsum('bhid,bhjd->bhij', q_, k_) * dec_, 0.0)
        v_new = u_ - jnp.einsum('bhcd,bhde->bhce', w_, state)
        o = (jnp.einsum('bhcd,bhde->bhce', q_ * jnp.exp(gc_)[..., None], state)
             + jnp.einsum('bhij,bhje->bhie', attn, v_new))
        g_last = gc_[..., -1:]
        state = (state * jnp.exp(g_last)[..., None]
                 + jnp.einsum('bhcd,bhce->bhde', k_ * jnp.exp(g_last - gc_)[..., None], v_new))
        return state, o

    init = jnp.zeros((b, h, dk, dv), jnp.float32)
    _, o = lax.scan(step, init, (qc, kc, u, w, gcum, decay))
    return from_chunks(o)

def hybrid_layer(h, mem, n_ffn1_pre, w_ffn1_gu, w_ffn1_down, n_ffn1_post, n_mix_pre, w_in,
                 gla_w_lr2, gla_b_lr, gla_norm, gdn_conv, gdn_a_log, gdn_dt_bias, gdn_norm,
                 mem_norm, w_mem_kv, w_up_gla, w_up_gdn, w_up_xa, w_out, n_mix_post,
                 n_ffn2_pre, w_ffn2_gu, w_ffn2_down, n_ffn2_post):
    f32 = jnp.float32
    bsz, s, _ = h.shape
    h = h + 0.5 * rmsnorm(swiglu(rmsnorm(h, n_ffn1_pre), w_ffn1_gu, w_ffn1_down), n_ffn1_post)

    u = rmsnorm(h, n_mix_pre)
    idx = [int(i) for i in np.cumsum(IN_SIZES)[:-1]]
    (gla_q, gla_k, gla_v, gla_lr, gla_r, gdn_qkv, gdn_b, gdn_a, gdn_z,
     xa_q, gate_logits) = jnp.split(u @ w_in, idx, axis=-1)

    q = gla_q.reshape(bsz, s, GLA_HEADS, GLA_DK).astype(f32) * (GLA_DK ** -0.5)
    k = gla_k.reshape(bsz, s, GLA_HEADS, GLA_DK).astype(f32)
    v = gla_v.reshape(bsz, s, GLA_HEADS, GLA_DV).astype(f32)
    logg = jax.nn.log_sigmoid((gla_lr @ gla_w_lr2 + gla_b_lr).astype(f32)) / GLA_TAU
    o = gla_chunked(q, k, v, logg.reshape(bsz, s, GLA_HEADS, GLA_DK))
    o = rmsnorm(o, gla_norm) * jax.nn.silu(gla_r.reshape(bsz, s, GLA_HEADS, GLA_DV).astype(f32))
    y_gla = o.reshape(bsz, s, GLA_V).astype(h.dtype) @ w_up_gla

    qkv = causal_short_conv(gdn_qkv, gdn_conv)
    q, k, v = jnp.split(qkv, [GDN_QK, 2 * GDN_QK], axis=-1)
    q = l2norm(q.reshape(bsz, s, GDN_HEADS, GDN_DK).astype(f32)) * (GDN_DK ** -0.5)
    k = l2norm(k.reshape(bsz, s, GDN_HEADS, GDN_DK).astype(f32))
    v = v.reshape(bsz, s, GDN_HEADS, GDN_DV).astype(f32)
    beta = jax.nn.sigmoid(gdn_b.astype(f32))
    g = -jnp.exp(gdn_a_log.astype(f32)) * jax.nn.softplus(gdn_a.astype(f32) + gdn_dt_bias.astype(f32))
    o = gdn_chunked(q, k, v, g, beta)
    o = rmsnorm(o, gdn_norm) * jax.nn.silu(gdn_z.reshape(bsz, s, GDN_HEADS, GDN_DV).astype(f32))
    y_gdn = o.reshape(bsz, s, GDN_V).astype(h.dtype) @ w_up_gdn

    mk, mv = jnp.split(rmsnorm(mem, mem_norm) @ w_mem_kv, 2, axis=-1)
    mk = mk.reshape(bsz, -1, XA_HEADS, XA_DH)
    mv = mv.reshape(bsz, -1, XA_HEADS, XA_DH)
    qx = xa_q.reshape(bsz, s, XA_HEADS, XA_DH)
    sc = jnp.einsum('bshd,bmhd->bhsm', qx, mk).astype(f32) * (XA_DH ** -0.5)
    pr = jax.nn.softmax(sc, axis=-1).astype(mv.dtype)
    o = jnp.einsum('bhsm,bmhd->bshd', pr, mv).reshape(bsz, s, XA_W)
    y_xa = o @ w_up_xa

    g_a, g_b, g_c = jnp.split(jax.nn.sigmoid(gate_logits), N_BRANCH, axis=-1)
    mixed = (g_a * y_gla + g_b * y_gdn + g_c * y_xa) @ w_out
    h = h + rmsnorm(mixed, n_mix_post)

    h = h + 0.5 * rmsnorm(swiglu(rmsnorm(h, n_ffn2_pre), w_ffn2_gu, w_ffn2_down), n_ffn2_post)
    return h

def setup_inputs(seed: int = 0) -> dict:
    key = jax.random.key(seed)
    ks = iter(list(jax.random.split(key, 40)))
    L = DEPTH

    def dense(shape, fan_in):
        return jax.random.normal(next(ks), shape, jnp.float32) * (fan_in ** -0.5)

    def gain(n):
        return 1.0 + 0.02 * jax.random.normal(next(ks), (L, n), jnp.float32)

    x = jax.random.normal(next(ks), (BATCH, SEQ, D_MODEL), jnp.float32)
    mem = jax.random.normal(next(ks), (BATCH, MEM_LEN, D_MODEL), jnp.float32)
    dt = jnp.exp(jax.random.uniform(next(ks), (L, GDN_HEADS), jnp.float32,
                                    jnp.log(1e-3), jnp.log(1e-1)))
    gdn_dt_bias = dt + jnp.log(-jnp.expm1(-dt))
    gdn_a_log = jnp.log(jax.random.uniform(next(ks), (L, GDN_HEADS), jnp.float32, 1.0, 16.0))
    return {
        "x": x,
        "mem": mem,
        "n_ffn1_pre": gain(D_MODEL),
        "w_ffn1_gu": dense((L, D_MODEL, 2 * D_FF), D_MODEL),
        "w_ffn1_down": dense((L, D_FF, D_MODEL), D_FF),
        "n_ffn1_post": gain(D_MODEL),
        "n_mix_pre": gain(D_MODEL),
        "w_in": dense((L, D_MODEL, W_IN_COLS), D_MODEL),
        "gla_w_lr2": dense((L, GLA_RANK, GLA_QK), GLA_RANK),
        "gla_b_lr": 0.1 * jax.random.normal(next(ks), (L, GLA_QK), jnp.float32),
        "gla_norm": gain(GLA_DV),
        "gdn_conv": dense((L, CONV_W, 2 * GDN_QK + GDN_V), CONV_W),
        "gdn_a_log": gdn_a_log,
        "gdn_dt_bias": gdn_dt_bias,
        "gdn_norm": gain(GDN_DV),
        "mem_norm": gain(D_MODEL),
        "w_mem_kv": dense((L, D_MODEL, 2 * XA_W), D_MODEL),
        "w_up_gla": dense((L, GLA_V, D_MODEL), GLA_V),
        "w_up_gdn": dense((L, GDN_V, D_MODEL), GDN_V),
        "w_up_xa": dense((L, XA_W, D_MODEL), XA_W),
        "w_out": dense((L, D_MODEL, D_MODEL), D_MODEL),
        "n_mix_post": gain(D_MODEL),
        "n_ffn2_pre": gain(D_MODEL),
        "w_ffn2_gu": dense((L, D_MODEL, 2 * D_FF), D_MODEL),
        "w_ffn2_down": dense((L, D_FF, D_MODEL), D_FF),
        "n_ffn2_post": gain(D_MODEL),
    }

def reference(x, mem, n_ffn1_pre, w_ffn1_gu, w_ffn1_down, n_ffn1_post, n_mix_pre, w_in,
              gla_w_lr2, gla_b_lr, gla_norm, gdn_conv, gdn_a_log, gdn_dt_bias, gdn_norm,
              mem_norm, w_mem_kv, w_up_gla, w_up_gdn, w_up_xa, w_out, n_mix_post,
              n_ffn2_pre, w_ffn2_gu, w_ffn2_down, n_ffn2_post):
    h = x
    for l in range(DEPTH):
        h = hybrid_layer(h, mem, n_ffn1_pre[l], w_ffn1_gu[l], w_ffn1_down[l], n_ffn1_post[l],
                         n_mix_pre[l], w_in[l], gla_w_lr2[l], gla_b_lr[l], gla_norm[l],
                         gdn_conv[l], gdn_a_log[l], gdn_dt_bias[l], gdn_norm[l],
                         mem_norm[l], w_mem_kv[l], w_up_gla[l], w_up_gdn[l], w_up_xa[l],
                         w_out[l], n_mix_post[l], n_ffn2_pre[l], w_ffn2_gu[l],
                         w_ffn2_down[l], n_ffn2_post[l])
    return h


_drawn_inputs = setup_inputs


def setup_inputs(seed=0):
    import zlib

    import numpy as np

    out = dict(_drawn_inputs(seed))
    spreads = {}
    factors = {'n_ffn1_pre': 2.868,
     'n_ffn1_post': 4.085,
     'gla_norm': 132.684,
     'gdn_norm': 132.445,
     'mem_norm': 29.717,
     'n_mix_post': 3.944,
     'n_ffn2_pre': 18.825,
     'n_ffn2_post': 93.76,
     'gla_b_lr': 2.807}
    for name, (base, spread) in spreads.items():
        noise = np.random.default_rng([zlib.crc32(name.encode()), seed]).standard_normal(out[name].shape)
        drawn = base * np.exp(spread * noise) if base else spread * noise
        out[name] = __import__('jax').numpy.asarray(drawn.astype(out[name].dtype))
    for name, factor in factors.items():
        out[name] = (out[name] * factor).astype(out[name].dtype)
    return out
```

```python
import math

import concourse.bass as bass
from concourse import mybir
from contextlib import ExitStack

D = 2048
SEQ = 256
P = 128
NT = SEQ // P
D_FF = ((8 * D // 3 + 255) // 256) * 256
CW = 512
UK = 2
RING = 4
LOOK = RING
EPS = 1e-6
GLA_H, GLA_DK, GLA_DV = 4, D // 16, D // 8
GLA_TAU = 16.0
GDN_H, GDN_D = 8, D // 16
XA_H, XA_D = 4, D // 8
GLA_QK, GLA_V, RANK = GLA_H * GLA_DK, GLA_H * GLA_DV, 16
GDN_W = GDN_H * GDN_D
XA_W = XA_H * XA_D
TAPS = 4
NEG = -1e30

IN_GQ = 0
IN_GK = IN_GQ + GLA_QK
IN_GV = IN_GK + GLA_QK
IN_LR = IN_GV + GLA_V
IN_GR = IN_LR + RANK
IN_DQ = IN_GR + GLA_V
IN_DK = IN_DQ + GDN_W
IN_DV = IN_DK + GDN_W
IN_B = IN_DV + GDN_W
IN_A = IN_B + GDN_H
IN_DZ = IN_A + GDN_H
IN_XQ = IN_DZ + GDN_W
IN_GATE = IN_XQ + XA_W

KT_D = D // P
KT_F = D_FF // P
KT_O = GLA_V // P
U_D, U_F, U_O = KT_D // UK, KT_F // UK, KT_O // UK
N_GU = D_FF // CW
NG = 4

PHASES = [("gu1", N_GU * 2 * U_D), ("down1", 4 * U_F), ("mem", 4 * U_D), ("proj", NG * 4 * U_D),
          ("gates0", 6 * U_D), ("up0", 6 * U_O), ("gates1", 6 * U_D), ("up1", 6 * U_O),
          ("out", 4 * U_D), ("gu2", N_GU * 2 * U_D), ("down2", 4 * U_F)]
CHUNKS = {"gu1": 2 * N_GU, "down1": 4, "mem": 4, "proj": 4 * NG, "gates0": 6, "up0": 6, "gates1": 6,
          "up1": 6, "out": 4, "gu2": 2 * N_GU, "down2": 4}
UB, QB = {}, {}
_u = _q = 0
for _name, _n in PHASES:
    UB[_name], QB[_name] = _u, _q
    _u += _n
    _q += CHUNKS[_name]
N_UNITS = _u

T_X, T_ACT1, T_MEM, T_U, T_M, T_H2, T_ACT2 = 0, 4, 15, 19, 23, 27, 31
R_X, R_MEM, R_D1, R_H1, R_OUT, R_H2, R_D2 = range(7)
LOADED = 48
LOG_SCALE = -0.5 * math.log(GDN_D)


def hybrid_layer(nc, a, out, h_dram, mk_dram, mv_dram):
    fp32 = mybir.dt.float32
    f32r = mybir.dt.float32r
    u32 = mybir.dt.uint32
    ALU = mybir.AluOpType
    ACT = mybir.ActivationFunctionType
    AXX = mybir.AxisListType.X
    ds = bass.ds

    with ExitStack() as ctx:
        def sb(name, shape, dt=fp32):
            return ctx.enter_context(nc.sbuf_tensor(name, shape, dt))

        def overlay(*groups):
            made = {}
            most, size = 0, {fp32: 4, f32r: 4}
            for group in groups:
                total = 0
                with ExitStack() as c:
                    for name, shape, dt in group:
                        made[name] = c.enter_context(nc.sbuf_tensor(name, shape, dt))
                        n = size[dt]
                        for s in shape[1:]:
                            n *= s
                        total += -(-n // 32) * 32
                most = max(most, total)
            sb("held_" + groups[0][0][0], [P, most // 4])
            return made

        sems = {}

        def sem(name):
            if name not in sems:
                sems[name] = ctx.enter_context(nc.semaphore(name))
            return sems[name]

        raw = sb("raw", [P, RING, UK, CW])
        whi = sb("whi", [P, RING, UK, CW], f32r)
        wlo = sb("wlo", [P, RING, UK, CW], f32r)
        ov = overlay(
            [("act_hi", [P, KT_F, SEQ], f32r), ("act_lo", [P, KT_F, SEQ], f32r)],
            [("u_hi", [P, KT_D, SEQ], f32r), ("u_lo", [P, KT_D, SEQ], f32r),
             ("o_hi", [P, 3, KT_O, SEQ], f32r), ("o_lo", [P, 3, KT_O, SEQ], f32r),
             ("msum", [P, NT, CW], fp32), ("mtmp", [P, NT, CW], fp32)],
            [("below", [P, 2 * KT_D, SEQ], fp32), ("mkn", [P, NT, CW], fp32), ("mvn", [P, NT, CW], fp32),
             ("mkT", [P, 4, SEQ], fp32), ("wsm", [P, KT_D, 32], fp32), ("wsmh", [P, KT_D, 32], f32r),
             ("wsml", [P, KT_D, 32], f32r)],
            [("below_post", [P, 80, SEQ], fp32), ("post_a", [P, 2, CW], fp32)],
            [("vec", [4 * KT_D + 4, P], fp32), ("convn", [TAPS * 24, P], fp32)])
        act_hi, act_lo, u_hi, u_lo = ov["act_hi"], ov["act_lo"], ov["u_hi"], ov["u_lo"]
        o_hi, o_lo, msum, mtmp = ov["o_hi"], ov["o_lo"], ov["msum"], ov["mtmp"]
        mkn, mvn, mkT, wsm, wsmh, wsml = (ov[k] for k in ("mkn", "mvn", "mkT", "wsm", "wsmh", "wsml"))
        vec, convn, post_a = ov["vec"], ov["convn"], ov["post_a"]
        U4 = [P, 4, P]
        ov = overlay(
            [("x_hi", [P, KT_D, SEQ], f32r), ("x_lo", [P, KT_D, SEQ], f32r)],
            [("sq", [P, 8, P], fp32), ("decT", U4, fp32), ("dec", U4, fp32), ("zb", U4, fp32),
             ("kbn", [P, 2, P], fp32), ("kend", [P, 2, P], fp32), ("qe", [P, 2, P], fp32),
             ("zg", [P, NT, 256], fp32), ("gqk", [P, 2, SEQ], fp32), ("cb", [P, NT, P], fp32),
             ("xqT", [P, 2, SEQ], fp32), ("ge", [P, 2, SEQ], fp32), ("gq", [P, 2, SEQ], fp32),
             ("att", [P, 2, NT, P], fp32), ("attx", [P, P], fp32), ("rg", [P, NT, 256], fp32),
             ("mkh", [P, 2, SEQ], fp32), ("mvh", [P, 2, 256], fp32)],
            [("post_b", [P, 2, CW], fp32)])
        x_hi, x_lo = ov["x_hi"], ov["x_lo"]
        posts = (post_a, post_a, ov["post_b"])
        sq, decT, dec, zb, kbn, kend, qe = (ov[k] for k in ("sq", "decT", "dec", "zb", "kbn", "kend", "qe"))
        zg, gqk, cb, xqT, ge, gq = (ov[k] for k in ("zg", "gqk", "cb", "xqT", "ge", "gq"))
        att, attx, rg, mkh, mvh = (ov[k] for k in ("att", "attx", "rg", "mkh", "mvh"))
        ov = overlay(
            [("nat", [P, NT, D], fp32), ("res", [P, 2, NT, CW], fp32)],
            [("pr", [P, 4, NT, CW], fp32), ("yr", [P, 10, SEQ], fp32)],
            [("gates", [P, 6, NT, CW], fp32)])
        nat, res, pr, yr, gates = (ov[k] for k in ("nat", "res", "pr", "yr", "gates"))
        conv = yr[:, 0:6, :]
        rn = yr[:, 6:10, :].rearrange("p a b -> p (a b)")
        lmat = yr[:, 6:8, :].rearrange("p a (b c) -> p (a b) c", c=P)
        attnT = yr[:, 8:10, :].rearrange("p a (b c) -> p (a b) c", c=P)
        vb = yr[:, 4:6, :].rearrange("p a (b c) -> p (a b) c", c=P)
        vnew = yr[:, 0:2, :].rearrange("p a (b c) -> p (a b) c", c=P)
        wTn = yr[:, 2, :].rearrange("p (b c) -> p b c", c=P)
        state = yr[:, 3, :].rearrange("p (b c) -> p b c", c=P)
        xinv, tinv = sq[:, 0:4, :], sq[:, 4:8, :]
        osq, og = decT, dec
        lsn = xqT[:, 0, :]
        lsl = xqT[:, 1, :]
        prob, probT = gq, ge
        ggo = gqk

        masks = sb("masks", [P, 8, P])
        ident = masks[:, 0, :]
        ones = sb("ones", [P, P])
        tri = sb("tri", [P, P])
        lowA = sb("lowA", [P, P])
        highB = sb("highB", [P, P])
        lev = masks[:, 1:8, :]
        vecT = sb("vecT", [P, 4 * KT_D + 4])
        convT = sb("convT", [P, TAPS, 3, GDN_H])
        gnorm = sb("gnorm", [P, GLA_DV])
        dnorm = sb("dnorm", [P, GDN_D])
        lr2g = sb("lr2g", [RANK, P])
        lrT = sb("lrT", [RANK, SEQ])
        small = sb("small", [P, NT, 32])
        alog = sb("alog", [P, GDN_H])
        dtb = sb("dtb", [P, GDN_H])
        st = sb("st", [P, 5, NT, GDN_H])
        stw = sb("stw", [P, 4, NT, GDN_H])
        gs = sb("gs", [P, 10, 2])
        cwg = sb("cwg", [P, TAPS * 3, 2])
        blr = sb("blr", [P, 1])
        cst = sb("cst", [P, 4])
        halfn = sb("halfn", [P, NT])
        ssp = sb("ssp", [P, 7, NT, 4])
        ssum = sb("ssum", [P, 7, NT])
        rs = sb("rs", [P, 7, NT])
        rsw = sb("rsw", [P, 7, NT])
        rsh = sb("rsh", [P, 7, NT])
        bias_c = sb("bias_c", [P, 1])
        mx = sb("mx", [P, 4, NT])
        oss = sb("oss", [P, 4])
        gss = sb("gss", [P, NT])
        junk = sb("junk", [P, CW], mybir.dt.bfloat16)

        acc = ctx.enter_context(nc.psum_tensor("acc", [P, 2, NT, CW], fp32))
        mix = ctx.enter_context(nc.psum_tensor("mix", [P, 4, CW], fp32))

        def m4(b):
            return mix[:, b, :].rearrange("p (u n) -> p u n", n=P)

        def m2(b):
            return mix[:, b, :].rearrange("p (u n) -> p u n", n=SEQ)

        def units(w):
            return w.rearrange("(u k p) n -> u p k n", k=UK, p=P)

        w_gu = [units(a["w_ffn1_gu"][0]), units(a["w_ffn2_gu"][0])]
        w_dn = [units(a["w_ffn1_down"][0]), units(a["w_ffn2_down"][0])]
        w_in, w_kv, w_o = units(a["w_in"][0]), units(a["w_mem_kv"][0]), units(a["w_out"][0])
        w_up = [units(a[k][0]) for k in ("w_up_gla", "w_up_gdn", "w_up_xa")]
        tok = lambda v: v.rearrange("(t p) n -> p t n", p=P)
        x_v, mem_v, out_v = tok(a["x"][0]), tok(a["mem"][0]), tok(out[0])
        h_v = tok(h_dram)
        mk_v = mk_dram.rearrange("(k p) m -> p k m", p=P)
        mv_v = tok(mv_dram)

        hi_ready, lo_ready, unit_used = sem("hi_ready"), sem("lo_ready"), sem("unit_used")
        raw_full = [sem(f"raw_full{s}") for s in range(RING)]
        acc_out = [sem("acc_out0"), sem("acc_out1")]
        t_done, t_hi, t_lo = sem("t_done"), sem("t_hi"), sem("t_lo")

        def at(base, i, per, j):
            return base + i * per + j

        def groups_done(eng, count):
            for name in ("gdn_lo", "gla_lo", "xa_lo"):
                eng.wait_ge(sem(name), count + 1)

        block = ctx.enter_context(nc.Block())

        @block.sync
        def _(sp):
            def load(n, j, pieces):
                s = j % RING
                if not isinstance(n, int) or n >= RING:
                    sp.wait_ge(lo_ready, n - RING + 1)
                col, left = 0, LOADED
                for src in pieces:
                    w = src.shape[-1]
                    inc = left if src is pieces[-1] else 16
                    left -= inc
                    sp.dma_start(raw[:, s, :, col:col + w], src).then_inc(raw_full[s], inc)
                    col += w

            def load_gu(f):
                def step(i):
                    for j in range(2 * U_D):
                        load(at(UB[f"gu{f + 1}"], i, 2 * U_D, j), j,
                             [w_gu[f][j % U_D][:, :, ds(i * CW + j // U_D * D_FF, CW)]])

                step(0)
                with sp.Fori(1, N_GU) as i:
                    step(i)

            def load_down(f):
                with sp.Fori(0, 2) as i:
                    for j in range(2 * U_F):
                        load(at(UB[f"down{f + 1}"], i, 2 * U_F, j), j,
                             [w_dn[f][j % U_F][:, :, ds(i * (2 * CW) + j // U_F * CW, CW)]])

            def load_gates(p):
                with sp.Fori(0, 2) as i:
                    for j in range(3 * U_D):
                        load(at(UB[f"gates{p}"], i, 3 * U_D, j), j,
                             [w_in[j % U_D][:, :, ds(i * CW + (IN_GATE + j // U_D * D + 2 * p * CW), CW)]])

            def load_up(p):
                with sp.Fori(0, 2) as i:
                    for j in range(3 * U_O):
                        load(at(UB[f"up{p}"], i, 3 * U_O, j), j,
                             [w_up[j // U_O][j % U_O][:, :, ds(i * CW + 2 * p * CW, CW)]])

            load_gu(0)
            load_down(0)
            with sp.Fori(0, 2) as i:
                for j in range(2 * U_D):
                    load(at(UB["mem"], i, 2 * U_D, j), j, [w_kv[j % U_D][:, :, ds(i * CW + j // U_D * XA_W, CW)]])
            with sp.Fori(0, NG) as g:
                for j in range(4 * U_D):
                    cols = [[(IN_DQ, 256), (IN_DK, 256)], [(IN_DV, 256), (IN_DZ, 256)],
                            [(IN_GQ, 128), (IN_GK, 128), (IN_GV, 256)], [(IN_GR, 256), (IN_XQ, 256)]][j // U_D]
                    load(at(UB["proj"], g, 4 * U_D, j), j,
                         [w_in[j % U_D][:, :, ds(g * w + o, w)] for o, w in cols])
            load_gates(0)
            load_up(0)
            load_gates(1)
            load_up(1)
            with sp.Fori(0, 4) as i:
                for j in range(U_D):
                    load(at(UB["out"], i, U_D, j), j, [w_o[j][:, :, ds(i * CW, CW)]])
            load_gu(1)
            load_down(1)

        @block.gpsimd
        def _(pl):
            made = [0]

            def const(ins):
                ins.then_inc(sem("consts"), 1)
                made[0] += 1
                pl.wait_ge(sem("consts"), made[0])

            def select(t, op, fill, base, pattern, mult):
                const(pl.affine_select(out=t, in_=t, compare_op=op, fill=fill, base=base,
                                       pattern=pattern, channel_multiplier=mult))

            rows = lambda v: v.rearrange("o (k p) -> (o k) p", p=P)
            for k, name in enumerate(("n_ffn1_pre", "n_mix_pre", "mem_norm", "n_ffn2_pre")):
                pl.dma_start(vec[k * KT_D:(k + 1) * KT_D, :], rows(a[name])).then_inc(sem("vecs_in"), 16)
            pl.dma_start(vec[4 * KT_D:4 * KT_D + 4, :], rows(a["gla_b_lr"])).then_inc(sem("vecs_in"), 16)
            pl.dma_start(convn[:, :], a["gdn_conv"][0].rearrange("s (k p) -> (s k) p", p=P)).then_inc(sem("vecs_in"), 16)
            const(pl.memset(ident[:, :], 0.0))
            select(ident[:, :], ALU.not_equal, 1.0, 0, [[-1, P]], 1)
            const(pl.memset(halfn[:, :], -0.5))
            const(pl.memset(cst[:, 1:2], EPS))
            const(pl.memset(cst[:, 2:3], LOG_SCALE))
            pl.memset(ones[:, :], 1.0).then_inc(sem("first_consts"), 1)
            const(pl.memset(tri[:, :], 1.0))
            select(tri[:, :], ALU.is_ge, 0.0, 0, [[1, P]], -1)
            const(pl.memset(lowA[:, :], 0.0))
            select(lowA[:, :], ALU.is_ge, NEG, 0, [[1, P]], -1)
            const(pl.memset(highB[:, :], 0.0))
            select(highB[:, :], ALU.is_gt, -NEG, 0, [[-1, P]], 1)
            const(pl.memset(lev[:, :, :], 0.0))
            for l in range(7):
                m = 1 << l
                upper = lev[:, l, :].rearrange("p (b h m) -> p b h m", h=2, m=m)[:, :, 1, :]
                nb = P // (2 * m)
                const(pl.memset(upper, 1.0))
                select(upper, ALU.is_ge, 0.0, 0, [[-2 * m, nb], [0, m]], 1)
                select(upper, ALU.is_ge, 0.0, m - 1, [[2 * m, nb], [0, m]], -1)
            pl.engine_nop().then_inc(sem("all_consts"), 1)
            for name in ("gdn_lo", "gla_lo", "xa_lo"):
                pl.engine_nop().then_inc(sem(name), 1)
            for dst, src in ((gnorm[:, :], a["gla_norm"].broadcast_to([P, GLA_DV])),
                             (dnorm[:, :], a["gdn_norm"].broadcast_to([P, GDN_D])),
                             (alog[:, :], a["gdn_a_log"].broadcast_to([P, GDN_H])),
                             (dtb[:, :], a["gdn_dt_bias"].broadcast_to([P, GDN_H]))):
                pl.dma_start(dst, src).then_inc(sem("small_in"), 16)

            def rsqrt(k, half=False):
                pl.wait_ge(sem("norm_sum"), k + 1)
                pl.tensor_scalar(rsw[:, k, :], ssum[:, k, :], 1.0 / D, EPS, ALU.mult, ALU.add).then_inc(sem("norm_mean"), 1)
                pl.wait_ge(sem("norm_mean"), k + 1)
                if not half:
                    pl.tensor_tensor(rs[:, k, :], rsw[:, k, :], halfn[:, :], ALU.pow).then_inc(sem("norm_rs"), 1)
                else:
                    pl.tensor_tensor(rsh[:, k, :], rsw[:, k, :], halfn[:, :], ALU.pow).then_inc(sem("norm_pow"), 1)
                    pl.wait_ge(sem("norm_pow"), 1 if k == R_D1 else 2)
                    pl.tensor_scalar(rs[:, k, :], rsh[:, k, :], 0.5, None, ALU.mult).then_inc(sem("norm_rs"), 1)

            def store_h(b, c):
                pl.wait_ge(sem("h_ready"), 4 * b + c + 1)
                dst = (h_v if b < 2 else out_v)[:, :, c * CW:(c + 1) * CW]
                pl.dma_start(dst, nat[:, :, c * CW:(c + 1) * CW]).then_inc(sem("h_stored"), 16)

            def fetch(b, c, src, post):
                n = 4 * b + c
                if b == 2:
                    pl.wait_ge(sem("h_stored"), 8 * 16)
                    pl.wait_ge(unit_used, UB["down2"])
                if b == 1:
                    pl.wait_ge(sem("h_stored"), 4 * 16)
                    pl.wait_ge(t_done, T_M + 4)
                if b == 0:
                    pl.wait_ge(unit_used, UB["mem"])
                if n >= 2:
                    pl.wait_ge(sem("h_ready"), n - 1)
                pl.dma_start(res[:, c % 2], src[:, :, c * CW:(c + 1) * CW]).then_inc(sem(f"res_in{c % 2}"), 16)
                pl.dma_start(posts[b][:, c % 2], post[:, c * CW:(c + 1) * CW].broadcast_to([P, CW])).then_inc(sem(f"res_in{c % 2}"), 16)

            def residual(b, k, half, src, post):
                fetch(b, 0, src, post)
                fetch(b, 1, src, post)
                rsqrt(k, half)
                for c in range(4):
                    store_h(b, c)
                    if c + 2 < 4:
                        fetch(b, c + 2, src, post)

            rsqrt(R_X)
            for c in range(4):
                if c >= 2:
                    pl.wait_ge(t_done, T_MEM + c - 1)
                    pl.wait_ge(sem("squared"), 8 * R_MEM + 2 * (c - 1))
                pl.dma_start(res[:, c % 2], mem_v[:, :, c * CW:(c + 1) * CW]).then_inc(sem(f"mem_in{c % 2}"), 16)
            rsqrt(R_MEM)
            pl.wait_ge(t_done, T_MEM + 4)
            residual(0, R_D1, True, x_v, a["n_ffn1_post"])
            rsqrt(R_H1)
            pl.wait_ge(unit_used, UB["mem"])
            w_all = a["w_in"][0].rearrange("(k p) n -> p k n", p=P)
            pl.dma_start(wsm[:, :, 0:RANK], w_all[:, :, IN_LR:IN_LR + RANK]).then_inc(sem("wsm_in"), 16)
            pl.dma_start(wsm[:, :, RANK:32], w_all[:, :, IN_B:IN_B + 2 * GDN_H]).then_inc(sem("wsm_in"), 16)
            for i in range(2):
                pl.wait_ge(sem("mk_ready"), i + 1)
                pl.dma_start(mk_v[:, 4 * i:4 * i + 4, :], mkT[:, :, :]).then_inc(sem("mk_stored"), 16)
                pl.wait_ge(acc_out[1], QB["mem"] // 2 + i + 1)
                pl.dma_start(mv_v[:, :, i * CW:(i + 1) * CW], mvn[:, :, :]).then_inc(sem("mv_stored"), 16)
            pl.wait_ge(sem("mk_stored"), 2 * 16)
            pl.wait_ge(sem("mv_stored"), 2 * 16)
            pl.wait_ge(unit_used, UB["proj"])
            with pl.Fori(0, NG) as g:
                groups_done(pl, g)
                pl.dma_start(mkh[:, :, :], mk_v[:, ds(g * 2, 2), :]).then_inc(sem("mkv_in"), 16)
                pl.dma_start(mvh[:, :, :], mv_v[:, :, ds(g * 256, 256)]).then_inc(sem("mkv_in"), 16)
                pl.dma_start(lr2g[:, :], a["gla_w_lr2"][0][:, ds(g * P, P)]).then_inc(sem("mkv_in"), 16)
                pl.memset(att[:, :, :, :], 0.0).then_inc(sem("att_zero"), 1)
                pl.wait_ge(sem("group_consts"), g * 3 + 3)
                pl.tensor_tensor(zb[:, :, :].rearrange("p (h t) n -> p h t n", t=NT),
                                 tri[:, :].unsqueeze(1).unsqueeze(1).broadcast_to([P, 2, NT, P]),
                                 gs[:, 0:NT, :].rearrange("p t h -> p h t").unsqueeze(3).broadcast_to([P, 2, NT, P]),
                                 ALU.mult).then_inc(sem("grhs_ready"), 1)
                pl.wait_ge(sem("silu_zr"), g + 1)
                zg4 = zg[:, :, :].rearrange("p t (h n) -> p (t h) n", h=2)
                pl.tensor_tensor(zg4, zg4, dnorm[:, :].unsqueeze(1).broadcast_to([P, 4, P]), ALU.mult).then_inc(sem("zg_ready"), 1)
                pl.tensor_tensor(rg[:, :, :], rg[:, :, :], gnorm[:, :].unsqueeze(1).broadcast_to([P, NT, 256]),
                                 ALU.mult).then_inc(sem("rg_ready"), 1)
            pl.wait_ge(acc_out[1], QB["out"] // 2)
            residual(1, R_OUT, False, h_v, a["n_mix_post"])
            rsqrt(R_H2)
            residual(2, R_D2, True, h_v, a["n_ffn2_post"])
            pl.wait_ge(sem("h_stored"), 12 * 16)

        @block.tensor
        def _(pe):
            def unit(n, j, hi, lo, k0, par, first, last, before):
                s = j % RING
                pe.wait_ge(lo_ready, n + 1)
                if first and (not isinstance(before, int) or before > 0):
                    pe.wait_ge(acc_out[par], before)
                for k in range(UK):
                    for t in range(NT):
                        cols = slice(t * P, (t + 1) * P)
                        for m, (x, w) in enumerate(((hi, whi), (hi, wlo), (lo, whi))):
                            ins = nc.tensor.matmul(acc[:, par, t, :], x[:, k0 + k, cols], w[:, s, k, :],
                                                   start=first and k == 0 and m == 0,
                                                   stop=last and k == UK - 1 and m == 2)
                ins.then_inc(unit_used, 1)

            def chunk(n0, j0, count, hi, lo, par, before, between=None):
                for j in range(count):
                    unit(n0 + j, j0 + j, hi, lo, UK * j, par, j == 0, j == count - 1, before)
                    if between is not None:
                        between(j0 + j)

            def transposed(tq, src, pair, free=0):
                if not isinstance(tq, int) or tq - free > 0:
                    pe.wait_ge(t_lo, tq - free)
                v = mix[:, 2 * pair:2 * pair + 2, :].rearrange("p b (k s) -> p (b k) s", s=SEQ)
                for blk in range(4):
                    for t in range(NT):
                        ins = nc.tensor.transpose(v[:, blk, t * P:(t + 1) * P], src[:, t, blk * P:(blk + 1) * P], ident[:, :])
                ins.then_inc(t_done, 1)

            def gu(f, i, first):
                base, q = UB[f"gu{f + 1}"], QB[f"gu{f + 1}"] // 2

                def between(j):
                    if j == 2 and not first:
                        pe.wait_ge(acc_out[1], q + i)
                        transposed((T_ACT1, T_ACT2)[f] - 1 + i, nat[:, :, CW:2 * CW], 0)
                    if first and j in (1, 3, 5):
                        if j < 5:
                            norm_chunk(f, (j + 3) // 2)
                        pe.wait_ge(t_lo, (T_X, T_H2)[f] + (j + 3) // 2)

                for half in range(2):
                    chunk(at(base, i, 2 * U_D, half * U_D), half * U_D, U_D, x_hi, x_lo, half, q + i, between)

            def norm_chunk(f, c):
                if f == 0:
                    pe.wait_ge(sem(f"x_in{c}"), 16)
                else:
                    pe.wait_ge(sem("h_ready"), 4 + c + 1)
                transposed((T_X, T_H2)[f] + c, nat[:, :, c * CW:(c + 1) * CW], c % 2, min(c, 1))

            def down(f):
                base, q = UB[f"down{f + 1}"], QB[f"down{f + 1}"] // 2

                def between(j):
                    if j == 2 and i == 0:
                        pe.wait_ge(acc_out[1], q)
                        transposed((T_ACT1, T_ACT2)[f] + N_GU - 1, nat[:, :, CW:2 * CW], 0)
                    if f == 0 and i == 0 and j in (3, 8, 13, 18):
                        c = (j - 3) // 5
                        pe.wait_ge(sem(f"mem_in{c % 2}"), 16 * (c // 2 + 1))
                        transposed(T_MEM + c, res[:, c % 2], c % 2)
                    if i == 0 and j == U_F - 3:
                        pe.wait_ge(t_lo, (T_ACT1, T_ACT2)[f] + N_GU)

                for i in range(2):
                    for half in range(2):
                        chunk(at(base, i, 2 * U_F, half * U_F), half * U_F, U_F, act_hi, act_lo, half, q + i, between)

            def memory():
                base, q = UB["mem"], QB["mem"] // 2

                def between(j):
                    j += 2 * U_D * i
                    if 2 <= j < 6:
                        c = j - 2
                        pe.wait_ge(sem("h_ready"), c + 1)
                        transposed(T_U + c, nat[:, :, c * CW:(c + 1) * CW], c % 2, min(c, 1))
                    if j in (9, 25):
                        pe.wait_ge(acc_out[0], q + j // 16 + 1)
                        pe.wait_ge(t_lo, T_U + 4)
                        if j == 25:
                            pe.wait_ge(sem("mk_ready"), 1)
                        v = mix[:, 2:4, :].rearrange("p b (k s) -> p (b k) s", s=SEQ)
                        for blk in range(4):
                            for t in range(NT):
                                ins = nc.tensor.transpose(v[:, blk, t * P:(t + 1) * P], mkn[:, t, blk * P:(blk + 1) * P], ident[:, :])
                        ins.then_inc(sem("mk_done"), 1)

                for i in range(2):
                    for half in range(2):
                        chunk(at(base, i, 2 * U_D, half * U_D), half * U_D, U_D, x_hi, x_lo, half, q + i, between)

            def small_steps(j):
                if j == 0:
                    pe.wait_ge(sem("wsm_lo"), 1)
                    for t in range(NT):
                        for k in range(KT_D):
                            cols = slice(t * P, (t + 1) * P)
                            for m, (x, w) in enumerate(((u_hi, wsmh), (u_hi, wsml), (u_lo, wsmh))):
                                ins = nc.tensor.matmul(mix[:, 0, t * 32:(t + 1) * 32], x[:, k, cols], w[:, k, :],
                                                       start=k == 0 and m == 0, stop=k == KT_D - 1 and m == 2)
                    ins.then_inc(sem("small_done"), 1)
                if j == 2:
                    pe.wait_ge(sem("small_out"), 1)
                    for t in range(NT):
                        ins = nc.tensor.transpose(mix[0:RANK, 1, t * P:(t + 1) * P], small[:, t, 0:RANK], ident[:, :])
                    ins.then_inc(sem("lrT_done"), 1)
                if j == 7:
                    pe.wait_ge(sem("logdecay"), 1)
                    av = st[:, 0].rearrange("p t h -> p (t h)")
                    nc.tensor.matmul(mix[:, 2, 0:16], tri[:, :], av, start=True, stop=True)
                    nc.tensor.matmul(mix[:, 2, 16:32], ones[:, :], av, start=True, stop=True).then_inc(sem("gsum_done"), 1)

            def mixer_steps(j, g):
                qp = QB["proj"] // 2
                E = lambda name, n=None: pe.wait_ge(sem(name), g + 1 if n is None else n)
                if j == 0:
                    groups_done(pe, g)
                    pe.wait_ge(acc_out[0], qp + g * 2 + 1)
                    pe.wait_ge(acc_out[1], qp + g * 2 + 1)
                    for b in range(3):
                        for h in range(2):
                            for t in range(NT):
                                o = (b % 2) * 256 + h * P
                                ins = nc.tensor.transpose(mix[:, b, h * SEQ + t * P:h * SEQ + (t + 1) * P],
                                                          pr[:, b // 2, t, o:o + P], ident[:, :])
                    ins.then_inc(sem("gdn_in"), 1)
                if j == 1:
                    E("grhs_ready")
                    nc.tensor.matmul(mix[:, 3, :], ones[:, :], zb[:, :, :].rearrange("p u n -> p (u n)"),
                                     start=True, stop=True).then_inc(sem("gsums_done"), 1)
                if j == 2:
                    E("qexp_ready")
                    E("dexp_ready")
                    pe.wait_ge(acc_out[1], qp + g * 2 + 2)
                    for b in range(2):
                        for t in range(NT):
                            ins = nc.tensor.transpose(m2(3)[:, b, t * P:(t + 1) * P],
                                                      pr[:, 3, t, 256 + b * P:256 + (b + 1) * P], ident[:, :])
                    ins.then_inc(sem("xa_in"), 1)
                if j == 3:
                    E("xq_ready")
                    pe.wait_ge(sem("mkv_in"), g * 48 + 48)
                    for t in range(NT):
                        for b in range(2):
                            ins = nc.tensor.matmul(m2(3)[:, t, :], xqT[:, b, t * P:(t + 1) * P], mkh[:, b, :],
                                                   start=b == 0, stop=b == 1)
                    ins.then_inc(sem("xa_scores"), 1)
                if j == 4:
                    E("sq_ready")
                    for b in range(2):
                        nc.tensor.matmul(mix[:, b, :], ones[:, :], sq[:, 4 * b:4 * b + 4, :].rearrange("p u n -> p (u n)"),
                                         start=True, stop=True)
                    for h in range(2):
                        for t in range(NT):
                            ins = nc.tensor.transpose(m4(2)[:, 2 * h + t, :], conv[:, 4 + h, t * P:(t + 1) * P], ident[:, :])
                    ins.then_inc(sem("ssq_done"), 1)
                if j == 6:
                    E("vb_ready")
                    for h in range(2):
                        for t in range(NT):
                            u, cols = 2 * h + t, slice(t * P, (t + 1) * P)
                            kt, qt = conv[:, 2 + h, cols], conv[:, h, cols]
                            nc.tensor.matmul(m4(2)[:, u, :], kt, kt, start=True, stop=True)
                            nc.tensor.matmul(m4(0)[:, u, :], kt, qt, start=True, stop=True)
                            ins = nc.tensor.transpose(m4(1)[:, u, :], kt, ident[:, :])
                    ins.then_inc(sem("kk_done"), 1)
                    E("prob_ready")
                    for mt in range(2):
                        for t in range(NT):
                            ins = nc.tensor.transpose(m2(3)[:, mt, t * P:(t + 1) * P], prob[:, t, mt * P:(mt + 1) * P], ident[:, :])
                    ins.then_inc(sem("xa_pT"), 1)
                if j == 7:
                    E("l_ready")
                    for u in range(4):
                        ins = nc.tensor.transpose(m4(0)[:, u, :], lmat[:, u, :], ident[:, :])
                    ins.then_inc(sem("lev_a"), 1)
                    E("probT_ready")
                    for b in range(2):
                        for mt in range(2):
                            ins = nc.tensor.matmul(m2(3)[:, b, :], mvh[:, mt, b * P:(b + 1) * P], probT[:, mt, :],
                                                   start=mt == 0, stop=mt == 1)
                    ins.then_inc(sem("xa_o"), 1)
                if j == 8:
                    E("kb_ready")
                    E("z_ready", g * 7 + 1)
                    for u in range(4):
                        ins = nc.tensor.transpose(m4(1)[:, u, :], zb[:, u, :], ident[:, :])
                    ins.then_inc(sem("lev_b"), 1)
                for l in range(1, 7):
                    if j == 7 + 2 * l:
                        E("xt_ready", g * 7 + l)
                        for u in range(4):
                            ins = nc.tensor.matmul(m4(0)[:, u, :], lmat[:, u, :], xinv[:, u, :], start=True, stop=True)
                        ins.then_inc(sem("lev_a"), 1)
                    if j == 8 + 2 * l:
                        E("z_ready", g * 7 + l + 1)
                        for u in range(4):
                            ins = nc.tensor.matmul(m4(1)[:, u, :], tinv[:, u, :], zb[:, u, :], start=True, stop=True)
                            if l < 6:
                                ins = nc.tensor.matmul(m4(2)[:, u, :], zb[:, u, :], tinv[:, u, :], start=True, stop=True)
                        ins.then_inc(sem("lev_b"), 1)
                if j == 9:
                    E("xa_lo", g + 2)
                    pe.wait_ge(acc_out[0], qp + g * 2 + 2)
                    for b in range(2):
                        for t in range(NT):
                            ins = nc.tensor.transpose(m2(3)[:, b, t * P:(t + 1) * P], pr[:, 2, t, b * P:(b + 1) * P], ident[:, :])
                    ins.then_inc(sem("gla_in"), 1)
                if j == 10:
                    E("gqk_ready")
                    nc.tensor.matmul(mix[:, 3, 0:SEQ], lr2g[:, :], lrT[:, :], start=True, stop=True).then_inc(sem("gla_lr"), 1)
                for n in range(4):
                    if j == 13 + 2 * n:
                        E("gqe_ready", g * 4 + n + 1)
                        if n:
                            E("att_ready", g * 4 + n)
                        for li in range(2):
                            for t in range(NT):
                                cols = slice(t * P, (t + 1) * P)
                                k_, q_ = (ge[:, li, cols], gq[:, li, cols]) if n or li else (gqk[:, 1, cols], gqk[:, 0, cols])
                                ins = nc.tensor.matmul(m4(3)[:, 2 * li + t, :], k_, q_, start=True, stop=True)
                        ins.then_inc(sem("gla_s"), 1)
                if j == 21:
                    E("gx_ready")
                    E("att_ready", g * 4 + 4)
                    nc.tensor.matmul(mix[:, 3, 0:P], gq[:, 0, P:2 * P], gq[:, 0, 0:P], start=True, stop=True).then_inc(sem("gla_x"), 1)
                if j == 21:
                    E("xt_ready", g * 7 + 7)
                    for h in range(2):
                        nc.tensor.matmul(m4(0)[:, h, :], xinv[:, 2 * h, :], vb[:, 2 * h, :], start=True, stop=True)
                        ins = nc.tensor.matmul(m4(2)[:, h, :], kbn[:, h, :], xinv[:, 2 * h + 1, :], start=True, stop=True)
                    ins.then_inc(sem("gdn_uw"), 1)
                if j == 22:
                    E("vn_ready", g * 2 + 1)
                    for h in range(2):
                        ins = nc.tensor.matmul(m4(1)[:, h, :], kend[:, h, :], vnew[:, 2 * h, :], start=True, stop=True)
                    ins.then_inc(sem("gdn_s"), 1)
                    E("attx_ready")
                    E("att_sum")
                    v = pr[:, 2, :, 256:512]
                    nc.tensor.matmul(m2(3)[:, 0, :], att[:, 0, 0, :], v[:, 0], start=True, stop=True)
                    nc.tensor.matmul(m2(3)[:, 1, :], att[:, 0, 1, :], v[:, 1], start=True, stop=False)
                    nc.tensor.matmul(m2(3)[:, 1, :], attx[:, :], v[:, 0], start=False, stop=True).then_inc(sem("gla_o"), 1)
                if j == 23:
                    E("wT_ready")
                    E("state_ready")
                    for h in range(2):
                        nc.tensor.matmul(m4(0)[:, h, :], xinv[:, 2 * h + 1, :], vb[:, 2 * h + 1, :], start=True, stop=False)
                        ins = nc.tensor.matmul(m4(0)[:, h, :], wTn[:, h, :], state[:, h, :], start=False, stop=True)
                    ins.then_inc(sem("gdn_v1"), 1)
                if j == 24:
                    E("vn_ready", g * 2 + 2)
                    for h in range(2):
                        nc.tensor.matmul(m4(2)[:, 2 * h, :], attnT[:, 2 * h, :], vnew[:, 2 * h, :], start=True, stop=True)
                        nc.tensor.matmul(m4(2)[:, 2 * h + 1, :], attnT[:, 2 * h + 1, :], vnew[:, 2 * h + 1, :], start=True, stop=False)
                        ins = nc.tensor.matmul(m4(2)[:, 2 * h + 1, :], qe[:, h, :], state[:, h, :], start=False, stop=True)
                    ins.then_inc(sem("gdn_o"), 1)
                if j == 26:
                    E("ggo_ready")
                    for b in range(2):
                        for t in range(NT):
                            ins = nc.tensor.transpose(m2(3)[:, b, t * P:(t + 1) * P], ggo[:, t, b * P:(b + 1) * P], ident[:, :])
                    ins.then_inc(sem("gla_oT"), 1)
                if j == 27:
                    E("og_ready")
                    for h in range(2):
                        for t in range(NT):
                            ins = nc.tensor.transpose(m2(0)[:, h, t * P:(t + 1) * P], og[:, 2 * h + t, :], ident[:, :])
                    ins.then_inc(sem("gdn_oT"), 1)

            def group(g, mixed):
                for c in range(4):
                    chunk(at(UB["proj"], g, 4 * U_D, c * U_D), c * U_D, U_D, u_hi, u_lo, c % 2,
                          QB["proj"] // 2 + g * 2 + c // 2, (lambda j: mixer_steps(j, mixed)) if mixed is not None else small_steps)

            def gate_logits(p, mixed):
                for k in range(6):
                    chunk(at(UB[f"gates{p}"], 0, 0, k * U_D), k * U_D, U_D, u_hi, u_lo, k % 2, QB[f"gates{p}"] // 2 + k // 2,
                          (lambda j: mixer_steps(j, mixed)) if mixed is not None else
                          (lambda j: mixture(2 * p - 1) if j == 1 else None))

            def mixture(n):
                pe.wait_ge(sem("m_ready"), n + 1)
                transposed(T_M + n, msum[:, :, :], 0)

            def up(p):
                groups_done(pe, NG)
                for n2 in range(2):
                    for br in range(3):
                        k = 3 * n2 + br
                        chunk(UB[f"up{p}"] + k * U_O, k * U_O, U_O, o_hi[:, br], o_lo[:, br], k % 2,
                              QB[f"up{p}"] // 2 + k // 2, lambda j: mixture(2 * p) if j == 13 else None)

            def output():
                def between(j):
                    if j == 1:
                        mixture(3)
                    if j == 5:
                        pe.wait_ge(t_lo, T_M + 4)
                pe.wait_ge(t_lo, T_M + 3)
                for c in range(4):
                    chunk(UB["out"] + c * U_D, c * U_D, U_D, x_hi, x_lo, c % 2, QB["out"] // 2 + c // 2, between)

            pe.wait_ge(sem("first_consts"), 1)
            pe.wait_ge(sem("vecs_in"), 6 * 16)
            nc.tensor.transpose(mix[:, 3, 0:4 * KT_D + 4], vec[:, :], ident[0:4 * KT_D + 4, 0:4 * KT_D + 4])
            nc.tensor.transpose(mix[:, 3, P:P + TAPS * 24], convn[:, :], ident[0:TAPS * 24, 0:TAPS * 24]).then_inc(sem("vecT_done"), 1)
            pe.wait_ge(sem("vecT_ready"), 2)
            norm_chunk(0, 0)
            norm_chunk(0, 1)
            pe.wait_ge(t_lo, T_X + 1)
            gu(0, 0, True)
            with pe.Fori(1, N_GU) as i:
                gu(0, i, False)
            down(0)
            memory()
            pe.wait_ge(t_lo, T_U + 4)
            pe.wait_ge(sem("all_consts"), 1)
            group(0, None)
            with pe.Fori(1, NG) as g:
                group(g, g - 1)
            gate_logits(0, NG - 1)
            up(0)
            gate_logits(1, None)
            up(1)
            output()
            norm_chunk(1, 0)
            norm_chunk(1, 1)
            pe.wait_ge(t_lo, T_H2 + 1)
            gu(1, 0, True)
            with pe.Fori(1, N_GU) as i:
                gu(1, i, False)
            down(1)

        @block.scalar
        def _(ac):
            act = nc.scalar.activation

            def split(n, per_i, j):
                s = j % RING
                i, n0, per = per_i
                m4_ = (n0 + LOOK) // RING + j // RING
                ac.wait_ge(raw_full[s], i * (per // RING * LOADED) + LOADED * (m4_ + 1))
                ac.wait_ge(unit_used, n + 1)
                act(whi[:, s], raw[:, s], ACT.Copy).then_inc(hi_ready, 1)

            def slots(n0, i, per, tasks, count=None, until=None):
                for j in range(per if count is None else count):
                    if until is None or j + LOOK < until:
                        split(at(n0, i, per, j), (i, n0, per), j)
                    tasks(j)

            def squares(k, c, src):
                for t in range(NT):
                    n = 8 * k + 2 * c + t
                    if n:
                        ac.wait_ge(sem("squared"), n)
                    act(junk[:, :], src[:, t, :], ACT.Square, accum_out=ssp[:, k, t, c:c + 1]).then_inc(sem("squared"), 1)

            def upper(tq, dst, pair, gain=None, scale=1.0):
                v = mix[:, 2 * pair:2 * pair + 2, :].rearrange("p b (k s) -> p (b k) s", s=SEQ)
                ac.wait_ge(t_done, tq + 1)
                if gain is None:
                    act(dst, v, ACT.Copy, scale=scale).then_inc(t_hi, 1)
                else:
                    for blk in range(4):
                        ins = act(dst[:, blk, :], v[:, blk, :], ACT.Copy, scale=vecT[:, gain + blk:gain + blk + 1])
                    ins.then_inc(t_hi, 1)

            def take_out(n, par, dst, k):
                ac.wait_ge(unit_used, n + 1)
                for t in range(NT):
                    ins = act(dst[:, t, :], acc[:, par, t, :], ACT.Copy, scale=rs[:, k, t:t + 1])
                ins.then_inc(acc_out[par], 1)

            def gu(f, i, first):
                n0, q = UB[f"gu{f + 1}"], QB[f"gu{f + 1}"] // 2

                def tasks(j):
                    if j == 2 and not first:
                        upper((T_ACT1, T_ACT2)[f] - 1 + i, act_hi[:, ds(i * 4 - 4, 4), :], 0)
                    if j == U_D - 1:
                        if first:
                            ac.wait_ge(sem("norm_rs"), (R_X, R_H2)[f] + 1)
                            ac.wait_ge(t_lo, (T_X, T_H2)[f] + 4)
                            if f == 1:
                                ac.wait_ge(sem("h_stored"), 8 * 16)
                        ac.wait_ge(unit_used, at(n0, i, 2 * U_D, j) + 1)
                        if not first:
                            ac.wait_ge(acc_out[1], q + i)
                        for t in range(NT):
                            ins = act(nat[:, t, 0:CW], acc[:, 0, t, :], ACT.Silu, scale=rs[:, (R_X, R_H2)[f], t:t + 1])
                        ins.then_inc(acc_out[0], 1)

                slots(n0, i, 2 * U_D, tasks)

            def down(f):
                n0, q = UB[f"down{f + 1}"], QB[f"down{f + 1}"] // 2

                def tasks(j):
                    if j == 2 and i == 0:
                        upper((T_ACT1, T_ACT2)[f] + N_GU - 1, act_hi[:, KT_F - 4:KT_F, :], 0)
                    if f == 0 and i == 0 and j in (3, 8, 13, 18):
                        c = (j - 3) // 5
                        ac.wait_ge(unit_used, UB["down1"])
                        upper(T_MEM + c, x_hi[:, 4 * c:4 * c + 4, :], c % 2, 2 * KT_D + 4 * c)
                        squares(R_MEM, c, res[:, c % 2])
                    if j % U_F == U_F - 1:
                        par = j // U_F
                        ac.wait_ge(acc_out[par], q + i + 1)
                        c = 2 * i + par
                        squares((R_D1, R_D2)[f], c, nat[:, :, c * CW:(c + 1) * CW])

                for i in range(2):
                    slots(n0, i, 2 * U_F, tasks, until=2 * U_F if (f, i) == (1, 1) else None)

            def memory():
                def tasks(j):
                    if 1 <= j < 5:
                        ac.wait_ge(sem("h_ready"), j)
                        squares(R_H1, j - 1, nat[:, :, (j - 1) * CW:j * CW])
                    if 2 <= j < 6:
                        c = j - 2
                        ac.wait_ge(unit_used, UB["mem"])
                        upper(T_U + c, u_hi[:, 4 * c:4 * c + 4, :], c % 2, KT_D + 4 * c)
                    if j % U_D == U_D - 1:
                        c = j // U_D
                        if c == 0:
                            ac.wait_ge(sem("norm_rs"), R_MEM + 1)
                        if c == 2:
                            ac.wait_ge(sem("mk_done"), 1)
                        if c == 3:
                            ac.wait_ge(sem("mv_stored"), 16)
                        take_out(UB["mem"] + j, c % 2, (mkn, mvn)[c % 2][:, :, :], R_MEM)
                    if j in (9, 25):
                        ac.wait_ge(sem("mk_done"), 1 + j // 16)
                        if j == 25:
                            ac.wait_ge(sem("mk_stored"), 16)
                        act(mkT[:, :, :], mix[:, 2:4, :].rearrange("p b (k s) -> p (b k) s", s=SEQ), ACT.Copy).then_inc(sem("mk_ready"), 1)
                slots(UB["mem"], 0, 4 * U_D, tasks)

            stc = [0]

            def st_step(ins):
                ins.then_inc(sem("st_act"), 1)
                stc[0] += 1
                ac.wait_ge(sem("st_act"), stc[0])

            def small_steps(j):
                if j == 1:
                    ac.wait_ge(sem("norm_rs"), R_H1 + 1)
                    ac.wait_ge(sem("small_done"), 1)
                    for t in range(NT):
                        ins = act(small[:, t, :], mix[:, 0, t * 32:(t + 1) * 32], ACT.Copy, scale=rs[:, R_H1, t:t + 1])
                    ins.then_inc(sem("small_out"), 1)
                    ac.wait_ge(sem("small_out"), 1)
                    act(stw[:, 0], small[:, :, RANK:RANK + GDN_H], ACT.Tanh, scale=0.5).then_inc(sem("tanh_b"), 1)
                if j == 2:
                    ac.wait_ge(sem("lrT_done"), 1)
                    act(lrT[:, :], mix[0:RANK, 1, 0:SEQ], ACT.Copy).then_inc(sem("lrT_ready"), 1)
                if j == 3:
                    ac.wait_ge(sem("a_bias"), 1)
                    st_step(act(stw[:, 2], stw[:, 1], ACT.Abs))
                    st_step(act(stw[:, 2], stw[:, 2], ACT.Exp, scale=-1.0))
                    st_step(act(alog[:, :], alog[:, :], ACT.Exp))
                    act(stw[:, 2], stw[:, 2], ACT.Ln, bias=1.0).then_inc(sem("softplus"), 1)
                if j == 8:
                    ac.wait_ge(sem("gsum_done"), 1)
                    act(stw[:, 3].rearrange("p t h -> p (t h)"), mix[:, 2, 0:16], ACT.Exp).then_inc(sem("exp_g"), 1)
                    ac.wait_ge(sem("g_rest"), 1)
                    act(st[:, 4], stw[:, 0], ACT.Exp).then_inc(sem("exp_rest"), 1)

            def mixer_steps(j, g):
                E = lambda name, n=None: ac.wait_ge(sem(name), g + 1 if n is None else n)
                qp = QB["proj"] // 2
                if j == 0:
                    groups_done(ac, g)
                    E("gdn_in")
                    E("group_consts", g * 3 + 3)
                    for b in range(3):
                        for h in range(2):
                            ins = act(conv[:, 2 * b + h, :], mix[:, b, h * SEQ:(h + 1) * SEQ], ACT.Copy,
                                      scale=cwg[:, 3 * (TAPS - 1) + b, h:h + 1])
                        ins.then_inc(sem("conv_seed"), 1)
                if j == 1:
                    E("gsums_done")
                    act(qe[:, :, :], mix[:, 3, :].rearrange("p (h t n) -> p h t n", t=NT, n=P)[:, :, 1, :], ACT.Exp).then_inc(sem("qexp_ready"), 1)
                if j == 2:
                    E("xa_in")
                    act(xqT[:, :, :], m2(3), ACT.Copy).then_inc(sem("xq_ready"), 1)
                    E("conv_done", g * 3 + 1)
                    act(conv[:, 0:2, :], conv[:, 0:2, :], ACT.Silu).then_inc(sem("conv_silu"), 1)
                if j == 3:
                    for b in range(1, 3):
                        E("conv_done", g * 3 + b + 1)
                        act(conv[:, 2 * b:2 * b + 2, :], conv[:, 2 * b:2 * b + 2, :], ACT.Silu).then_inc(sem("conv_silu"), 1)
                    E("conv_silu", g * 3 + 3)
                    act(sq[:, :, :], conv[:, 0:4, :].rearrange("p a (b n) -> p (a b) n", n=P), ACT.Square).then_inc(sem("sq_ready"), 1)
                    act(zg[:, :, :], pr[:, 1, :, 256:512], ACT.Silu)
                    act(rg[:, :, :], pr[:, 3, :, 0:256], ACT.Silu).then_inc(sem("silu_zr"), 1)
                if j == 4:
                    E("ssq_done")
                    act(rn, mix[:, 0:2, :].rearrange("p b n -> p (b n)"), ACT.Ln, bias=cst[:, 1:2]).then_inc(sem("rn_log"), 1)
                    E("rn_log")
                    act(rn[:, 0:CW], rn[:, 0:CW], ACT.Exp, scale=-0.5, bias=cst[:, 2:3])
                    act(rn[:, CW:2 * CW], rn[:, CW:2 * CW], ACT.Exp, scale=-0.5).then_inc(sem("rn_ready"), 1)
                    E("xa_nb")
                    for t in range(NT):
                        ins = act(prob[:, t, :], m2(3)[:, t, :], ACT.Exp, scale=XA_D ** -0.5, bias=mx[:, 1, t:t + 1],
                                  accum_out=mx[:, 2, t:t + 1])
                    ins.then_inc(sem("xa_exp"), 1)
                    E("dexp_ready")
                    act(decT[:, :, :], decT[:, :, :], ACT.Exp)
                    act(dec[:, :, :], dec[:, :, :], ACT.Exp, scale=-1.0).then_inc(sem("dec_ready"), 1)
                if j == 6:
                    E("kk_done")
                    for h in range(2):
                        act(kend[:, h, :], m4(1)[:, 2 * h, :], ACT.Copy, scale=gs[:, 8, h:h + 1])
                        ins = act(kbn[:, h, :], m4(1)[:, 2 * h + 1, :], ACT.Copy, scale=gs[:, 7, h:h + 1])
                    ins.then_inc(sem("kb_ready"), 1)
                    E("xa_pT")
                    act(probT[:, :, :], m2(3), ACT.Copy).then_inc(sem("probT_ready"), 1)
                if j == 7:
                    E("xa_o")
                    act(o_hi[:, 2, ds(g * 2, 2), :], m2(3), ACT.Copy).then_inc(sem("xa_hi"), 1)
                if j == 9:
                    E("gla_in")
                    act(gqk[:, 0, :], m2(3)[:, 0, :], ACT.Copy, scale=GLA_DK ** -0.5)
                    act(gqk[:, 1, :], m2(3)[:, 1, :], ACT.Copy).then_inc(sem("gqk_ready"), 1)
                if j == 10:
                    E("gla_lr")
                    act(lsl, mix[:, 3, 0:SEQ], ACT.Abs, bias=blr[:, 0:1]).then_inc(sem("lsl"), 1)
                    E("lsl", g * 2 + 1)
                    act(lsl, lsl, ACT.Exp, scale=-1.0).then_inc(sem("lsl"), 1)
                    E("lsl", g * 2 + 2)
                    act(lsl, lsl, ACT.Ln, bias=1.0).then_inc(sem("lsl_ready"), 1)
                for n in range(4):
                    if j == 11 + 2 * n:
                        lo = 1 if n == 0 else 0
                        E("gd_ready", g * 4 + n + 1)
                        act(ge[:, lo:2, :], ge[:, lo:2, :], ACT.Abs).then_inc(sem("gabs"), 1)
                        E("gabs", g * 4 + n + 1)
                        act(ge[:, lo:2, :], ge[:, lo:2, :], ACT.Exp, scale=-1.0 / GLA_TAU).then_inc(sem("gexp"), 1)
                if j == 19:
                    E("gla_s", g * 4 + 4)
                    act(bias_c[:, :], cb[:, 0, P - 1:P], ACT.Copy, scale=1.0 / GLA_TAU).then_inc(sem("bias_c"), 1)
                    E("bias_c")
                    act(ge[:, 0, 0:P], cb[:, 1, :], ACT.Exp, scale=1.0 / GLA_TAU)
                    act(ge[:, 0, P:2 * P], cb[:, 0, :], ACT.Exp, scale=-1.0 / GLA_TAU, bias=bias_c[:, 0:1]).then_inc(sem("gxe_ready"), 1)
                if j == 21:
                    E("gla_x")
                    act(attx[:, :], mix[:, 3, 0:P], ACT.Copy).then_inc(sem("attx_ready"), 1)
                    E("gdn_uw")
                    act(wTn, m4(2)[:, 0:2, :], ACT.Copy).then_inc(sem("wT_ready"), 1)
                if j == 22:
                    E("gdn_s")
                    act(state, m4(1)[:, 0:2, :], ACT.Copy).then_inc(sem("state_ready"), 1)
                    E("gla_o")
                    act(gq[:, :, :], m2(3), ACT.Square).then_inc(sem("gsq_ready"), 1)
                if j == 24:
                    E("gss_ready")
                    act(gss[:, :], gss[:, :], ACT.Ln, scale=1.0 / GLA_DV, bias=cst[:, 1:2]).then_inc(sem("gln"), 1)
                    E("gln")
                    act(gss[:, :], gss[:, :], ACT.Exp, scale=-0.5).then_inc(sem("grn_ready"), 1)
                    E("gdn_o")
                    act(osq[:, :, :], m4(2), ACT.Square).then_inc(sem("osq_ready"), 1)
                if j == 25:
                    E("oss_ready")
                    act(oss[:, :], oss[:, :], ACT.Ln, scale=1.0 / GDN_D, bias=cst[:, 1:2]).then_inc(sem("oln"), 1)
                    E("oln")
                    act(oss[:, :], oss[:, :], ACT.Exp, scale=-0.5).then_inc(sem("orn_ready"), 1)
                if j == 26:
                    E("gla_oT")
                    act(o_hi[:, 0, ds(g * 2, 2), :], m2(3), ACT.Copy).then_inc(sem("gla_hi"), 1)
                if j == 27:
                    E("gdn_oT")
                    act(o_hi[:, 1, ds(g * 2, 2), :], m2(0), ACT.Copy).then_inc(sem("gdn_hi"), 1)

            def free_chunk(c, mixed):
                if c < 4:
                    for name in (("gdn_in",), ("gdn_in", "silu_zr"), ("gla_in", "gla_o"), ("xa_in", "silu_zr"))[c]:
                        ac.wait_ge(sem(name), mixed + 1)
                else:
                    groups_done(ac, mixed + 1)

            def group(g, mixed):
                def tasks(j):
                    if mixed is None:
                        small_steps(j)
                    else:
                        mixer_steps(j, mixed)
                    if j % U_D == U_D - 1:
                        c = j // U_D
                        if mixed is None and c == 0:
                            ac.wait_ge(sem("h_stored"), 4 * 16)
                            ac.wait_ge(t_lo, T_U + 4)
                        elif mixed is not None:
                            free_chunk(c, mixed)
                        take_out(at(UB["proj"], g, 4 * U_D, j), c % 2, pr[:, c], R_H1)
                slots(UB["proj"], g, 4 * U_D, tasks)

            def gate_logits(p, mixed):
                def tasks(j):
                    if mixed is not None:
                        mixer_steps(j, mixed)
                    elif j == 1:
                        mixture(2 * p - 1)
                    if j % U_D == U_D - 1:
                        k = j // U_D
                        if mixed is not None:
                            free_chunk(k, mixed)
                        elif k == 0:
                            ac.wait_ge(sem("m_ready"), 2 * p)
                        take_out(UB[f"gates{p}"] + j, k % 2, gates[:, k], R_H1)
                slots(UB[f"gates{p}"], 0, 6 * U_D, tasks)

            def mixture(n):
                upper(T_M + n, x_hi[:, 4 * n:4 * n + 4, :], 0, scale=0.5)

            def up(p):
                def tasks(j):
                    if j % U_O == 0:
                        k = j // U_O
                        if k == 0:
                            ac.wait_ge(acc_out[1], QB[f"gates{p}"] // 2 + 3)
                        act(gates[:, k], gates[:, k], ACT.Tanh, scale=0.5).then_inc(sem("gate_ready"), 1)
                    if j == 13:
                        mixture(2 * p)
                slots(UB[f"up{p}"], 0, 6 * U_O, tasks)

            def output():
                def tasks(j):
                    if j == 1:
                        mixture(3)
                    if j % U_D == U_D - 1:
                        c = j // U_D
                        ac.wait_ge(acc_out[c % 2], QB["out"] // 2 + c // 2 + 1)
                        squares(R_OUT, c, nat[:, :, c * CW:(c + 1) * CW])
                slots(UB["out"], 0, 4 * U_D, tasks)

            for c in range(4):
                ac.dma_start(nat[:, :, c * CW:(c + 1) * CW], x_v[:, :, c * CW:(c + 1) * CW]).then_inc(sem(f"x_in{c}"), 16)
            ac.wait_ge(sem("first_consts"), 1)
            ac.wait_ge(sem("vecT_done"), 1)
            act(vecT[:, :], mix[:, 3, 0:4 * KT_D + 4], ACT.Copy).then_inc(sem("vecT_ready"), 1)
            act(convT[:, :, :, :].rearrange("p a b c -> p (a b c)"), mix[:, 3, P:P + TAPS * 24], ACT.Copy).then_inc(sem("vecT_ready"), 1)
            ac.wait_ge(sem("vecT_ready"), 2)
            for s in range(RING):
                if s == 2:
                    upper(T_X, x_hi[:, 0:4, :], 0, 0)
                ac.wait_ge(raw_full[s], LOADED)
                act(whi[:, s], raw[:, s], ACT.Copy).then_inc(hi_ready, 1)
            for c in range(1, 4):
                upper(T_X + c, x_hi[:, 4 * c:4 * c + 4, :], c % 2, 4 * c)
            for c in range(4):
                ac.wait_ge(sem(f"x_in{c}"), 16)
                squares(R_X, c, nat[:, :, c * CW:(c + 1) * CW])
            gu(0, 0, True)
            with ac.Fori(1, N_GU) as i:
                gu(0, i, False)
            down(0)
            memory()
            ac.wait_ge(sem("small_in"), 4 * 16)
            ac.wait_ge(sem("wsm_in"), 2 * 16)
            act(wsmh[:, :, :], wsm[:, :, :], ACT.Copy).then_inc(sem("wsm_hi"), 1)
            group(0, None)
            with ac.Fori(1, NG) as g:
                group(g, g - 1)
            gate_logits(0, NG - 1)
            up(0)
            gate_logits(1, None)
            up(1)
            output()
            for c in range(4):
                upper(T_H2 + c, x_hi[:, 4 * c:4 * c + 4, :], c % 2, 3 * KT_D + 4 * c)
                squares(R_H2, c, nat[:, :, c * CW:(c + 1) * CW])
            gu(1, 0, True)
            with ac.Fori(1, N_GU) as i:
                gu(1, i, False)
            down(1)

        @block.vector
        def _(ve):
            tt, stt, ts = nc.vector.tensor_tensor, nc.vector.scalar_tensor_tensor, nc.vector.tensor_scalar

            def split(n, j):
                s = j % RING
                ve.wait_ge(hi_ready, n + LOOK + 1)
                tt(wlo[:, s], raw[:, s], whi[:, s].bitcast(fp32), ALU.subtract).then_inc(lo_ready, 1)

            def slots(n0, i, per, tasks, until=None):
                for j in range(per):
                    if until is None or j + LOOK < until:
                        split(at(n0, i, per, j), j)
                    tasks(j)

            def lower(tq, dst, dst_hi, pair, gain=None, scale=None):
                v = mix[:, 2 * pair:2 * pair + 2, :].rearrange("p b (k s) -> p (b k) s", s=SEQ)
                ve.wait_ge(t_hi, tq + 1)
                hi = dst_hi.bitcast(fp32)
                if gain is not None:
                    for blk in range(4):
                        ins = stt(dst[:, blk, :], v[:, blk, :], vecT[:, gain + blk:gain + blk + 1], hi[:, blk, :], ALU.mult, ALU.subtract)
                elif scale is not None:
                    ins = stt(dst, v, scale, hi, ALU.mult, ALU.subtract)
                else:
                    ins = tt(dst, v, hi, ALU.subtract)
                ins.then_inc(t_lo, 1)

            def norm_sum(k):
                ve.wait_ge(sem("squared"), 8 * k + 8)
                nc.vector.tensor_reduce(ssum[:, k, :], ssp[:, k], AXX, ALU.add).then_inc(sem("norm_sum"), 1)

            def residual(b, k, c):
                if c == 0:
                    ve.wait_ge(sem("norm_rs"), k + 1)
                ve.wait_ge(sem(f"res_in{c % 2}"), 32 * (2 * b + c // 2 + 1))
                cs = slice(c * CW, (c + 1) * CW)
                for t in range(NT):
                    ins = stt(nat[:, t, cs], nat[:, t, cs], rs[:, k, t:t + 1], posts[b][:, c % 2], ALU.mult, ALU.mult)
                ins.then_inc(sem("normed"), 1)
                ve.wait_ge(sem("normed"), 4 * b + c + 1)
                tt(nat[:, :, cs], nat[:, :, cs], res[:, c % 2], ALU.add).then_inc(sem("h_ready"), 1)

            def gu(f, i, first):
                n0, q = UB[f"gu{f + 1}"], QB[f"gu{f + 1}"] // 2
                k = (R_X, R_H2)[f]

                def tasks(j):
                    if j == 2 and not first:
                        rows = ds(i * 4 - 4, 4)
                        lower((T_ACT1, T_ACT2)[f] - 1 + i, act_lo[:, rows, :], act_hi[:, rows, :], 0)
                    if j == 2 * U_D - 1:
                        ve.wait_ge(unit_used, at(n0, i, 2 * U_D, j) + 1)
                        ve.wait_ge(acc_out[0], q + i + 1)
                        ve.wait_ge(t_done, (T_ACT1, T_ACT2)[f] + i)
                        for t in range(NT):
                            ins = stt(nat[:, t, CW:2 * CW], acc[:, 1, t, :], rs[:, k, t:t + 1], nat[:, t, 0:CW], ALU.mult, ALU.mult)
                        ins.then_inc(acc_out[1], 1)

                slots(n0, i, 2 * U_D, tasks)

            def take_product(n, par, before, c):
                ve.wait_ge(unit_used, n + 1)
                nc.vector.tensor_copy(nat[:, :, c * CW:(c + 1) * CW], acc[:, par]).then_inc(acc_out[par], 1)

            def down(f):
                n0, q = UB[f"down{f + 1}"], QB[f"down{f + 1}"] // 2

                def tasks(j):
                    if j == 2 and i == 0:
                        lower((T_ACT1, T_ACT2)[f] + N_GU - 1, act_lo[:, KT_F - 4:KT_F, :], act_hi[:, KT_F - 4:KT_F, :], 0)
                    if f == 0 and i == 0 and j in (3, 8, 13, 18):
                        c = (j - 3) // 5
                        rows = slice(4 * c, 4 * c + 4)
                        lower(T_MEM + c, x_lo[:, rows, :], x_hi[:, rows, :], c % 2, 2 * KT_D + 4 * c)
                    if f == 0 and i == 0 and j == 19:
                        norm_sum(R_MEM)
                    if j % U_F == U_F - 1:
                        take_product(at(n0, i, 2 * U_F, j), j // U_F, None, 2 * i + j // U_F)

                for i in range(2):
                    slots(n0, i, 2 * U_F, tasks, 2 * U_F if (f, i) == (1, 1) else None)

            def memory():
                def tasks(j):
                    if j == 0:
                        norm_sum(R_D1)
                    if 1 <= j < 5:
                        residual(0, R_D1, j - 1)
                    if 2 <= j < 6:
                        c = j - 2
                        rows = slice(4 * c, 4 * c + 4)
                        lower(T_U + c, u_lo[:, rows, :], u_hi[:, rows, :], c % 2, KT_D + 4 * c)
                    if j == 6:
                        norm_sum(R_H1)
                slots(UB["mem"], 0, 4 * U_D, tasks)

            def small_steps(j):
                if j == 1:
                    ve.wait_ge(sem("tanh_b"), 1)
                    ts(st[:, 2], stw[:, 0], 0.5, 0.5, ALU.mult, ALU.add).then_inc(sem("beta"), 1)
                    tt(stw[:, 1], small[:, :, RANK + GDN_H:32], dtb[:, :].unsqueeze(1).broadcast_to([P, NT, GDN_H]),
                       ALU.add).then_inc(sem("a_bias"), 1)
                if j == 4:
                    ve.wait_ge(sem("softplus"), 1)
                    stt(stw[:, 2], stw[:, 1], 0.0, stw[:, 2], ALU.max, ALU.add).then_inc(sem("softplus_sum"), 1)
                    ve.wait_ge(sem("softplus_sum"), 1)
                    stt(st[:, 0], stw[:, 2], -1.0, alog[:, :].unsqueeze(1).broadcast_to([P, NT, GDN_H]), ALU.mult,
                        ALU.mult).then_inc(sem("logdecay"), 1)
                if j == 8:
                    ve.wait_ge(sem("exp_g"), 1)
                    nc.vector.tensor_copy(st[:, 1].rearrange("p t h -> p (t h)"), mix[:, 2, 0:16]).then_inc(sem("g_out"), 1)
                    ve.wait_ge(sem("g_out"), 1)
                    ve.wait_ge(sem("beta"), 1)
                    tt(stw[:, 0], mix[:, 2, 16:32].rearrange("p (t h) -> p t h", t=NT), st[:, 1], ALU.subtract).then_inc(sem("g_rest"), 1)
                    stt(st[:, 3], st[:, 2], -1.0, stw[:, 3], ALU.mult, ALU.mult).then_inc(sem("neg_beta"), 1)
                    ve.wait_ge(sem("neg_beta"), 1)
                    ve.wait_ge(sem("exp_rest"), 1)

            def mixer_steps(j, g):
                E = lambda name, n=None: ve.wait_ge(sem(name), g + 1 if n is None else n)

                def conv_taps(b):
                    E("conv_seed", g * 3 + b + 1)
                    for s in range(1, TAPS):
                        if s > 1:
                            E("conv_tap", g * 6 + 2 * b + s - 1)
                        for h in range(2):
                            y = conv[:, 2 * b + h, s:SEQ]
                            ins = stt(y, mix[:, b, h * SEQ:(h + 1) * SEQ - s], cwg[:, 3 * (TAPS - 1 - s) + b, h:h + 1], y,
                                      ALU.mult, ALU.add)
                        ins.then_inc(sem("conv_tap" if s < TAPS - 1 else "conv_done"), 1)

                if j == 0:
                    groups_done(ve, g)
                    nc.vector.tensor_copy(gs[:, :, :], st[:, :, :, ds(g * 2, 2)].rearrange("p a t h -> p (a t) h")).then_inc(sem("group_consts"), 1)
                    nc.vector.tensor_copy(cwg[:, :, :], convT[:, :, :, ds(g * 2, 2)].rearrange("p a b h -> p (a b) h")).then_inc(sem("group_consts"), 1)
                    nc.vector.tensor_copy(blr[:, :], vecT[:, ds(g + 4 * KT_D, 1)]).then_inc(sem("group_consts"), 1)
                    conv_taps(0)
                if j == 1:
                    E("qexp_ready")
                    E("group_consts", g * 3 + 3)
                    for h in range(2):
                        for t in range(NT):
                            u = 2 * h + t
                            stt(decT[:, u, :], m4(3)[:, u, :], gs[:, 2 + t, h:h + 1], lowA[:, :], ALU.subtract, ALU.min)
                            ins = stt(dec[:, u, :], m4(3)[:, u, :], gs[:, 2 + t, h:h + 1], highB[:, :], ALU.subtract, ALU.max)
                    ins.then_inc(sem("dexp_ready"), 1)
                    conv_taps(1)
                if j == 2:
                    conv_taps(2)
                if j == 4:
                    E("xa_scores")
                    nc.vector.tensor_reduce(mx[:, 0, :], m2(3), AXX, ALU.max).then_inc(sem("xa_max"), 1)
                    E("xa_max")
                    ts(mx[:, 1, :], mx[:, 0, :], -(XA_D ** -0.5), None, ALU.mult).then_inc(sem("xa_nb"), 1)
                if j == 5:
                    E("rn_ready")
                    cv = conv[:, 0:4, :].rearrange("p a b -> p (a b)")
                    tt(cv, cv, rn, ALU.mult)
                    E("ssq_done")
                    for h in range(2):
                        for t in range(NT):
                            u = 2 * h + t
                            ins = ts(vb[:, u, :], m4(2)[:, u, :], gs[:, 4 + t, h:h + 1], None, ALU.mult)
                    ins.then_inc(sem("vb_ready"), 1)
                    E("xa_exp")
                    nc.vector.reciprocal(mx[:, 3, :], mx[:, 2, :]).then_inc(sem("xa_rec"), 1)
                    E("xa_rec")
                    for t in range(NT):
                        ins = ts(prob[:, t, :], prob[:, t, :], mx[:, 3, t:t + 1], None, ALU.mult)
                    ins.then_inc(sem("prob_ready"), 1)
                if j == 6:
                    E("kk_done")
                    E("dec_ready")
                    for h in range(2):
                        for t in range(NT):
                            u = 2 * h + t
                            stt(lmat[:, u, :], m4(2)[:, u, :], gs[:, 4 + t, h:h + 1], dec[:, u, :], ALU.mult, ALU.mult)
                    tt(attnT, m4(0), decT[:, :, :], ALU.mult).then_inc(sem("l_ready"), 1)
                    E("qexp_ready")
                    tt(qe[:, :, :], conv[:, 0:2, P:2 * P], qe[:, :, :], ALU.mult).then_inc(sem("qe_ready"), 1)
                for n in range(4):
                    if j == 13 + 2 * n:
                        E("gla_s", g * 4 + n + 1)
                        if n == 0:
                            E("att_zero")
                        else:
                            E("att_ready", g * 4 + n)
                for l in range(7):
                    mask = lev[:, l, :].unsqueeze(1).broadcast_to([P, 4, P])
                    if j == 7 + 2 * l:
                        E("lev_a", g * 7 + l + 1)
                        tt(zb[:, :, :], m4(0), mask, ALU.mult).then_inc(sem("z_ready"), 1)
                    if j == 8 + 2 * l:
                        E("lev_b", g * 7 + l + 1)
                        eye = ident[:, :].unsqueeze(1).broadcast_to([P, 4, P])
                        if l == 0:
                            E("z_ready", g * 7 + 1)
                            tt(xinv, eye, zb[:, :, :], ALU.subtract)
                            tt(tinv, eye, m4(1), ALU.subtract).then_inc(sem("xt_ready"), 1)
                        elif l < 6:
                            E("xt_ready", g * 7 + l)
                            tt(xinv, xinv, m4(1), ALU.subtract)
                            tt(tinv, tinv, m4(2), ALU.subtract).then_inc(sem("xt_ready"), 1)
                        else:
                            tt(xinv, xinv, m4(1), ALU.subtract).then_inc(sem("xt_ready"), 1)
                if j == 8:
                    E("xa_hi")
                    tt(o_lo[:, 2, ds(g * 2, 2), :], m2(3), o_hi[:, 2, ds(g * 2, 2), :].bitcast(fp32), ALU.subtract).then_inc(sem("xa_lo"), 1)
                if j == 10:
                    E("lsl", g * 2 + 1)
                    ts(lsn, mix[:, 3, 0:SEQ], blr[:, 0:1], 0.0, ALU.add, ALU.min).then_inc(sem("lsn_ready"), 1)
                if j == 11:
                    E("lsl_ready")
                    E("lsn_ready")
                    for t in range(NT):
                        cols = slice(t * P, (t + 1) * P)
                        ins = nc.vector.tensor_tensor_scan(cb[:, t, :], lsn[:, cols], lsl[:, cols], 0.0, ALU.add, ALU.subtract)
                    ins.then_inc(sem("cb_ready"), 1)
                    E("cb_ready")
                for n in range(4):
                    levels = ((1, 0),) if n == 0 else ((0, 2 * n - 1), (1, 2 * n))
                    if j == 11 + 2 * n:
                        for li, l in levels:
                            m = 1 << l
                            v = cb[:, :, :].rearrange("p t n -> p (t n)").rearrange("p (b m) -> p b m", m=2 * m)
                            ins = tt(ge[:, li, :].rearrange("p (b m) -> p b m", m=2 * m), v,
                                     v[:, :, m - 1:m].broadcast_to([P, SEQ // (2 * m), 2 * m]), ALU.subtract)
                        ins.then_inc(sem("gd_ready"), 1)
                    if j == 13 + 2 * n:
                        nc.vector.copy_predicated(
                            att[:, :, :, :], masks[:, 2 * n:2 * n + 2, :].bitcast(u32).unsqueeze(2).broadcast_to([P, 2, NT, P]),
                            mix[:, 3, :].rearrange("p (l t n) -> p l t n", l=2, t=NT)).then_inc(sem("att_ready"), 1)
                    if j == 12 + 2 * n:
                        E("gexp", g * 4 + n + 1)
                        lo = levels[0][0]
                        qb = gqk[:, 0, :].unsqueeze(1).broadcast_to([P, 2 - lo, SEQ])
                        kb = gqk[:, 1, :].unsqueeze(1).broadcast_to([P, 2 - lo, SEQ])
                        tt(gq[:, lo:2, :], qb, ge[:, lo:2, :], ALU.mult)
                        tt(ge[:, lo:2, :], kb, ge[:, lo:2, :], ALU.mult).then_inc(sem("gqe_ready"), 1)
                if j == 20:
                    E("att_ready", g * 4 + 4)
                    tt(att[:, 0], att[:, 0], att[:, 1], ALU.add).then_inc(sem("att_sum"), 1)
                    E("gxe_ready")
                    tt(gq[:, 0, 0:P], gqk[:, 0, P:2 * P], ge[:, 0, 0:P], ALU.mult)
                    tt(gq[:, 0, P:2 * P], gqk[:, 1, 0:P], ge[:, 0, P:2 * P], ALU.mult).then_inc(sem("gx_ready"), 1)
                vn4 = vnew.rearrange("p (h t) n -> p h t n", t=NT)
                if j == 21:
                    E("gdn_uw")
                    nc.vector.tensor_copy(vn4[:, :, 0, :], m4(0)[:, 0:2, :]).then_inc(sem("vn_ready"), 1)
                if j == 23:
                    E("gdn_v1")
                    nc.vector.tensor_copy(vn4[:, :, 1, :], m4(0)[:, 0:2, :]).then_inc(sem("vn_ready"), 1)
                    E("gsq_ready")
                    nc.vector.tensor_reduce(gss[:, :], gq[:, :, :], AXX, ALU.add).then_inc(sem("gss_ready"), 1)
                if j == 24:
                    E("osq_ready")
                    nc.vector.tensor_reduce(oss[:, :], osq[:, :, :], AXX, ALU.add).then_inc(sem("oss_ready"), 1)
                if j == 25:
                    E("grn_ready")
                    E("rg_ready")
                    for t in range(NT):
                        ins = stt(ggo[:, t, :], m2(3)[:, t, :], gss[:, t:t + 1], rg[:, t, :], ALU.mult, ALU.mult)
                    ins.then_inc(sem("ggo_ready"), 1)
                    E("orn_ready")
                    E("zg_ready")
                    for h in range(2):
                        for t in range(NT):
                            u = 2 * h + t
                            ins = stt(og[:, u, :], m4(2)[:, u, :], oss[:, u:u + 1], zg[:, t, h * P:(h + 1) * P], ALU.mult, ALU.mult)
                    ins.then_inc(sem("og_ready"), 1)
                if j == 26:
                    E("gla_hi")
                    tt(o_lo[:, 0, ds(g * 2, 2), :], m2(3), o_hi[:, 0, ds(g * 2, 2), :].bitcast(fp32), ALU.subtract).then_inc(sem("gla_lo"), 1)
                if j == 27:
                    E("gdn_hi")
                    tt(o_lo[:, 1, ds(g * 2, 2), :], m2(0), o_hi[:, 1, ds(g * 2, 2), :].bitcast(fp32), ALU.subtract).then_inc(sem("gdn_lo"), 1)

            def group(g, mixed):
                slots(UB["proj"], g, 4 * U_D, small_steps if mixed is None else (lambda j: mixer_steps(j, mixed)))

            def gate_logits(p, mixed):
                slots(UB[f"gates{p}"], 0, 6 * U_D, (lambda j: mixer_steps(j, mixed)) if mixed is not None else
                      (lambda j: mixture(2 * p - 1) if j == 1 else None))

            def mixture(n):
                rows = slice(4 * n, 4 * n + 4)
                lower(T_M + n, x_lo[:, rows, :], x_hi[:, rows, :], 0, scale=0.5)

            def up(p):
                def tasks(j):
                    if j % U_O == U_O - 1:
                        k = j // U_O
                        n, br = 2 * p + k // 3, k % 3
                        ve.wait_ge(unit_used, UB[f"up{p}"] + j + 1)
                        ve.wait_ge(sem("gate_ready"), 6 * p + k + 1)
                        if br == 0:
                            ve.wait_ge(t_done, T_M + n)
                            stt(msum[:, :, :], gates[:, k], 1.0, acc[:, k % 2], ALU.add, ALU.mult).then_inc(acc_out[k % 2], 1)
                        else:
                            stt(mtmp[:, :, :], gates[:, k], 1.0, acc[:, k % 2], ALU.add, ALU.mult).then_inc(acc_out[k % 2], 1)
                            ve.wait_ge(acc_out[k % 2], QB[f"up{p}"] // 2 + k // 2 + 1)
                            ve.wait_ge(acc_out[(k - 1) % 2], QB[f"up{p}"] // 2 + (k - 1) // 2 + 1)
                            tt(msum[:, :, :], msum[:, :, :], mtmp[:, :, :], ALU.add).then_inc(sem("m_part" if br == 1 else "m_ready"), 1)
                            ve.wait_ge(sem("m_part" if br == 1 else "m_ready"), n + 1)
                    if j == 13:
                        mixture(2 * p)
                slots(UB[f"up{p}"], 0, 6 * U_O, tasks)

            def output():
                def tasks(j):
                    if j == 1:
                        mixture(3)
                    if j % U_D == U_D - 1:
                        take_product(UB["out"] + j, j // U_D % 2, None, j // U_D)
                slots(UB["out"], 0, 4 * U_D, tasks)

            for s in range(RING):
                if s == 2:
                    ve.wait_ge(sem("vecT_ready"), 2)
                    lower(T_X, x_lo[:, 0:4, :], x_hi[:, 0:4, :], 0, 0)
                ve.wait_ge(hi_ready, s + 1)
                tt(wlo[:, s], raw[:, s], whi[:, s].bitcast(fp32), ALU.subtract).then_inc(lo_ready, 1)
            for c in range(1, 4):
                lower(T_X + c, x_lo[:, 4 * c:4 * c + 4, :], x_hi[:, 4 * c:4 * c + 4, :], c % 2, 4 * c)
            norm_sum(R_X)
            ve.wait_ge(sem("norm_rs"), R_X + 1)
            gu(0, 0, True)
            with ve.Fori(1, N_GU) as i:
                gu(0, i, False)
            down(0)
            memory()
            ve.wait_ge(sem("wsm_hi"), 1)
            tt(wsml[:, :, :], wsm[:, :, :], wsmh[:, :, :].bitcast(fp32), ALU.subtract).then_inc(sem("wsm_lo"), 1)
            group(0, None)
            with ve.Fori(1, NG) as g:
                group(g, g - 1)
            gate_logits(0, NG - 1)
            up(0)
            gate_logits(1, None)
            up(1)
            output()
            norm_sum(R_OUT)
            residual(1, R_OUT, 0)
            for c in range(4):
                if c < 3:
                    residual(1, R_OUT, c + 1)
                lower(T_H2 + c, x_lo[:, 4 * c:4 * c + 4, :], x_hi[:, 4 * c:4 * c + 4, :], c % 2, 3 * KT_D + 4 * c)
            norm_sum(R_H2)
            ve.wait_ge(sem("norm_rs"), R_H2 + 1)
            gu(1, 0, True)
            with ve.Fori(1, N_GU) as i:
                gu(1, i, False)
            down(1)
            norm_sum(R_D2)
            for c in range(4):
                residual(2, R_D2, c)


_INS = ["x", "mem", "n_ffn1_pre", "w_ffn1_gu", "w_ffn1_down", "n_ffn1_post", "n_mix_pre", "w_in", "gla_w_lr2",
        "gla_b_lr", "gla_norm", "gdn_conv", "gdn_a_log", "gdn_dt_bias", "gdn_norm", "mem_norm", "w_mem_kv",
        "w_up_gla", "w_up_gdn", "w_up_xa", "w_out", "n_mix_post", "n_ffn2_pre", "w_ffn2_gu", "w_ffn2_down",
        "n_ffn2_post"]


def kernel(**inputs):
    import numpy as _np
    import concourse.bacc as _bacc
    from concourse import mybir as _mybir
    from concourse.bass_utils import run_bass_kernel_spmd as _run

    nc = _bacc.Bacc("TRN2", target_bir_lowering=False, num_devices=1)
    f32 = _mybir.dt.float32
    arrays, aps = {}, {}
    for name in _INS:
        arr = _np.ascontiguousarray(inputs[name])
        arrays[name] = arr
        aps[name] = nc.dram_tensor(name, arr.shape, _mybir.dt.from_np(arr.dtype), kind="ExternalInput").ap()
    out = nc.dram_tensor("out", (1, SEQ, D), f32, kind="ExternalOutput").ap()
    h = nc.dram_tensor("h_scratch", (SEQ, D), f32, kind="Internal").ap()
    mk = nc.dram_tensor("mk_scratch", (XA_W, SEQ), f32, kind="Internal").ap()
    mv = nc.dram_tensor("mv_scratch", (SEQ, XA_W), f32, kind="Internal").ap()
    hybrid_layer(nc, aps, out, h, mk, mv)
    r = _run(nc, [arrays], core_ids=[0])
    return r.results[0]["out"]
```

```python
import math

import concourse.bass as bass
from concourse import mybir
from contextlib import ExitStack


D = 2048
SEQ = 256
P = 128
NT = SEQ // P
D_FF = ((8 * D // 3 + 255) // 256) * 256
CW = 512
UK = 2
RING = 4
LOOK = RING
EPS = 1e-6
GLA_H, GLA_DK, GLA_DV = 4, D // 16, D // 8
GLA_TAU = 16.0
GDN_H, GDN_D = 8, D // 16
XA_H, XA_D = 4, D // 8
GLA_QK, GLA_V, RANK = GLA_H * GLA_DK, GLA_H * GLA_DV, 16
GDN_W = GDN_H * GDN_D
XA_W = XA_H * XA_D
TAPS = 4
NEG = -1e30

IN_GQ = 0
IN_GK = IN_GQ + GLA_QK
IN_GV = IN_GK + GLA_QK
IN_LR = IN_GV + GLA_V
IN_GR = IN_LR + RANK
IN_DQ = IN_GR + GLA_V
IN_DK = IN_DQ + GDN_W
IN_DV = IN_DK + GDN_W
IN_B = IN_DV + GDN_W
IN_A = IN_B + GDN_H
IN_DZ = IN_A + GDN_H
IN_XQ = IN_DZ + GDN_W
IN_GATE = IN_XQ + XA_W

KT_D = D // P
KT_F = D_FF // P
KT_O = GLA_V // P
U_D, U_F, U_O = KT_D // UK, KT_F // UK, KT_O // UK
N_GU = D_FF // CW
NG = 4

PHASES = [("gu1", N_GU * 2 * U_D), ("down1", 4 * U_F), ("mem", 4 * U_D), ("proj", NG * 4 * U_D),
          ("gates0", 6 * U_D), ("up0", 6 * U_O), ("gates1", 6 * U_D), ("up1", 6 * U_O),
          ("out", 4 * U_D), ("gu2", N_GU * 2 * U_D), ("down2", 4 * U_F)]
CHUNKS = {"gu1": 2 * N_GU, "down1": 4, "mem": 4, "proj": 4 * NG, "gates0": 6, "up0": 6, "gates1": 6,
          "up1": 6, "out": 4, "gu2": 2 * N_GU, "down2": 4}
UB, QB = {}, {}
_u = _q = 0
for _name, _n in PHASES:
    UB[_name], QB[_name] = _u, _q
    _u += _n
    _q += CHUNKS[_name]
N_UNITS = _u

STEP_AT = ([0, 1, None, 2, 3, 4, 5, None] + list(range(6, 26)) + [None, 26, 27] + 32 * [None])
TAKE_AT = [U_D - 1, 2 * U_D - 1, STEP_AT.index(22) + 2, 4 * U_D - 1, 5 * U_D - 1, 6 * U_D - 1]

T_X, T_ACT1, T_MEM, T_U, T_M, T_H2, T_ACT2 = 0, 4, 15, 19, 23, 27, 31
R_X, R_MEM, R_D1, R_H1, R_OUT, R_H2, R_D2 = range(7)
LOADED = 48
SPLIT_SMALL = 20
LOG_SCALE = -0.5 * math.log(GDN_D)


def hybrid_layer(nc, a, out, h_dram, mk_dram, mv_dram):
    fp32 = mybir.dt.float32
    f32r = mybir.dt.float32r
    u32 = mybir.dt.uint32
    ALU = mybir.AluOpType
    ACT = mybir.ActivationFunctionType
    AXX = mybir.AxisListType.X
    ds = bass.ds

    with ExitStack() as ctx:
        def sb(name, shape, dt=fp32):
            return ctx.enter_context(nc.sbuf_tensor(name, shape, dt))

        def overlay(*groups):
            made = {}
            most, size = 0, {fp32: 4, f32r: 4}
            for group in groups:
                total = 0
                with ExitStack() as c:
                    for name, shape, dt in group:
                        made[name] = c.enter_context(nc.sbuf_tensor(name, shape, dt))
                        n = size[dt]
                        for s in shape[1:]:
                            n *= s
                        total += -(-n // 32) * 32
                most = max(most, total)
            sb("held_" + groups[0][0][0], [P, most // 4])
            return made

        sems = {}

        def sem(name):
            if name not in sems:
                sems[name] = ctx.enter_context(nc.semaphore(name))
            return sems[name]

        raw = sb("raw", [P, RING, UK, CW])
        whi = sb("whi", [P, RING, UK, CW], f32r)
        wlo = sb("wlo", [P, RING, UK, CW], f32r)
        ov = overlay(
            [("act_hi", [P, KT_F, SEQ], f32r), ("act_lo", [P, KT_F, SEQ], f32r)],
            [("u_hi", [P, KT_D, SEQ], f32r), ("u_lo", [P, KT_D, SEQ], f32r),
             ("o_hi", [P, 3, KT_O, SEQ], f32r), ("o_lo", [P, 3, KT_O, SEQ], f32r),
             ("msum", [P, NT, CW], fp32), ("mtmp", [P, NT, CW], fp32)],
            [("below", [P, 2 * KT_D, SEQ], fp32), ("mkn", [P, NT, CW], fp32), ("mvn", [P, NT, CW], fp32),
             ("mkT", [P, 4, SEQ], fp32), ("wsm", [P, KT_D, 32], fp32), ("wsmh", [P, KT_D, 32], f32r),
             ("wsml", [P, KT_D, 32], f32r), ("small_T", [32, SEQ], fp32)],
            [("below_post", [P, 80, SEQ], fp32), ("post_a", [P, 2, CW], fp32)],
            [("res_mix", [P, NT, D], fp32), ("post_mix", [P, D], fp32)],
            [("vec", [4 * KT_D + 4, P], fp32), ("convn", [TAPS * 24, P], fp32)])
        act_hi, act_lo, u_hi, u_lo = ov["act_hi"], ov["act_lo"], ov["u_hi"], ov["u_lo"]
        o_hi, o_lo, msum, mtmp = ov["o_hi"], ov["o_lo"], ov["msum"], ov["mtmp"]
        mkn, mvn, mkT, wsm, wsmh, wsml = (ov[k] for k in ("mkn", "mvn", "mkT", "wsm", "wsmh", "wsml"))
        small_T, vec, convn, post_a = ov["small_T"], ov["vec"], ov["convn"], ov["post_a"]
        res_mix, post_mix = ov["res_mix"], ov["post_mix"]
        U4 = [P, 4, P]
        ov = overlay(
            [("x_hi", [P, KT_D, SEQ], f32r), ("x_lo", [P, KT_D, SEQ], f32r)],
            [("sq", [P, 8, P], fp32), ("decT", U4, fp32), ("dec", U4, fp32), ("zb", U4, fp32),
             ("kbn", [P, 2, P], fp32), ("kend", [P, 2, P], fp32), ("qe", [P, 2, P], fp32),
             ("zg", [P, NT, 256], fp32), ("gqk", [P, 2, SEQ], fp32), ("cb", [P, NT, P], fp32),
             ("xqT", [P, 2, SEQ], fp32), ("ge", [P, 2, SEQ], fp32), ("gq", [P, 2, SEQ], fp32),
             ("att", [P, 2, NT, P], fp32), ("attx", [P, P], fp32), ("rg", [P, NT, 256], fp32),
             ("mkh", [P, 2, SEQ], fp32), ("mvh", [P, 2, 256], fp32)],
            [("res_ffn2", [P, NT, D], fp32), ("post_ffn2", [P, D], fp32)])
        x_hi, x_lo = ov["x_hi"], ov["x_lo"]
        block_res, block_post = (None, res_mix, ov["res_ffn2"]), (None, post_mix, ov["post_ffn2"])
        sq, decT, dec, zb, kbn, kend, qe = (ov[k] for k in ("sq", "decT", "dec", "zb", "kbn", "kend", "qe"))
        zg, gqk, cb, xqT, ge, gq = (ov[k] for k in ("zg", "gqk", "cb", "xqT", "ge", "gq"))
        att, attx, rg, mkh, mvh = (ov[k] for k in ("att", "attx", "rg", "mkh", "mvh"))
        ov = overlay(
            [("nat", [P, NT, D], fp32), ("res", [P, 2, NT, CW], fp32)],
            [("pr", [P, 4, NT, CW], fp32), ("yr", [P, 10, SEQ], fp32)],
            [("gates", [P, 6, NT, CW], fp32)])
        nat, res, pr, yr, gates = (ov[k] for k in ("nat", "res", "pr", "yr", "gates"))
        conv = yr[:, 0:6, :]
        rn = yr[:, 6:10, :].rearrange("p a b -> p (a b)")
        lmat = yr[:, 6:8, :].rearrange("p a (b c) -> p (a b) c", c=P)
        attnT = yr[:, 8:10, :].rearrange("p a (b c) -> p (a b) c", c=P)
        vb = yr[:, 4:6, :].rearrange("p a (b c) -> p (a b) c", c=P)
        vnew = yr[:, 0:2, :].rearrange("p a (b c) -> p (a b) c", c=P)
        wTn = yr[:, 2, :].rearrange("p (b c) -> p b c", c=P)
        state = yr[:, 3, :].rearrange("p (b c) -> p b c", c=P)
        xinv, tinv = sq[:, 0:4, :], sq[:, 4:8, :]
        osq, og = decT, dec
        lsn = xqT[:, 0, :]
        lsl = xqT[:, 1, :]
        prob, probT = gq, ge
        ggo = gqk

        masks = sb("masks", [P, 8, P])
        ident = masks[:, 0, :]
        ones = sb("ones", [P, P])
        tri = sb("tri", [P, P])
        lowA = sb("lowA", [P, P])
        highB = sb("highB", [P, P])
        lev = masks[:, 1:8, :]
        vecT = sb("vecT", [P, 4 * KT_D + 4])
        convT = sb("convT", [P, TAPS, 3, GDN_H])
        gnorm = sb("gnorm", [P, GLA_DV])
        dnorm = sb("dnorm", [P, GDN_D])
        lr2g = sb("lr2g", [RANK, P])
        lrT = sb("lrT", [RANK, SEQ])
        small = sb("small", [P, NT, 32])
        alog = sb("alog", [P, GDN_H])
        dtb = sb("dtb", [P, GDN_H])
        st = sb("st", [P, 5, NT, GDN_H])
        stw = sb("stw", [P, 4, NT, GDN_H])
        gs = sb("gs", [P, 10, 2])
        cwg = sb("cwg", [P, TAPS * 3, 2])
        blr = sb("blr", [P, 1])
        cst = sb("cst", [P, 2])
        halfn = sb("halfn", [P, NT])
        ssp = sb("ssp", [P, 7, NT, 4])
        ssum = sb("ssum", [P, 7, NT])
        rsw = sb("rsw", [P, 7, NT])
        rs = sb("rs", [P, 7, NT])
        bias_c = sb("bias_c", [P, 1])
        mx = sb("mx", [P, 4, NT])
        oss = sb("oss", [P, 4])
        gss = sb("gss", [P, NT])
        junk = sb("junk", [P, CW], mybir.dt.bfloat16)

        acc = ctx.enter_context(nc.psum_tensor("acc", [P, 2, NT, CW], fp32))
        mix = ctx.enter_context(nc.psum_tensor("mix", [P, 4, CW], fp32))

        def m4(b):
            return mix[:, b, :].rearrange("p (u n) -> p u n", n=P)

        def m2(b):
            return mix[:, b, :].rearrange("p (u n) -> p u n", n=SEQ)

        def units(w):
            return w.rearrange("(u k p) n -> u p k n", k=UK, p=P)

        w_gu = [units(a["w_ffn1_gu"][0]), units(a["w_ffn2_gu"][0])]
        w_dn = [units(a["w_ffn1_down"][0]), units(a["w_ffn2_down"][0])]
        w_in, w_kv, w_o = units(a["w_in"][0]), units(a["w_mem_kv"][0]), units(a["w_out"][0])
        w_up = [units(a[k][0]) for k in ("w_up_gla", "w_up_gdn", "w_up_xa")]
        tok = lambda v: v.rearrange("(t p) n -> p t n", p=P)
        x_v, mem_v, out_v = tok(a["x"][0]), tok(a["mem"][0]), tok(out[0])
        h_v = tok(h_dram)
        mk_v = mk_dram.rearrange("(k p) m -> p k m", p=P)
        mv_v = tok(mv_dram)

        hi_ready, lo_ready, unit_used = sem("hi_ready"), sem("lo_ready"), sem("unit_used")
        raw_full = [sem(f"raw_full{s}") for s in range(RING)]
        acc_out = [sem("acc_out0"), sem("acc_out1")]
        t_done, t_hi, t_lo = sem("t_done"), sem("t_hi"), sem("t_lo")

        def half_tiles(count):
            return 2 * count

        def at(base, i, per, j):
            return base + i * per + j

        def groups_done(eng, count):
            for name in ("gdn_lo", "gla_lo", "xa_lo"):
                eng.wait_ge(sem(name), count + 1)

        block = ctx.enter_context(nc.Block())

        @block.sync
        def _(sp):
            def load(n, j, pieces):
                s = j % RING
                if not isinstance(n, int) or n >= RING:
                    sp.wait_ge(lo_ready, n - RING + 1)
                col, left = 0, LOADED
                for src in pieces:
                    w = src.shape[-1]
                    inc = left if src is pieces[-1] else 16
                    left -= inc
                    sp.dma_start(raw[:, s, :, col:col + w], src).then_inc(raw_full[s], inc)
                    col += w

            def load_gu(f):
                def step(i):
                    for j in range(2 * U_D):
                        load(at(UB[f"gu{f + 1}"], i, 2 * U_D, j), j,
                             [w_gu[f][j % U_D][:, :, ds(i * CW + j // U_D * D_FF, CW)]])

                step(0)
                with sp.Fori(1, N_GU) as i:
                    step(i)

            def load_down(f):
                with sp.Fori(0, 2) as i:
                    for j in range(2 * U_F):
                        load(at(UB[f"down{f + 1}"], i, 2 * U_F, j), j,
                             [w_dn[f][j % U_F][:, :, ds(i * (2 * CW) + j // U_F * CW, CW)]])

            def load_gates(p):
                with sp.Fori(0, 2) as i:
                    for j in range(3 * U_D):
                        load(at(UB[f"gates{p}"], i, 3 * U_D, j), j,
                             [w_in[j % U_D][:, :, ds(i * CW + (IN_GATE + j // U_D * D + 2 * p * CW), CW)]])

            def load_up(p):
                with sp.Fori(0, 2) as i:
                    for j in range(3 * U_O):
                        load(at(UB[f"up{p}"], i, 3 * U_O, j), j,
                             [w_up[j // U_O][j % U_O][:, :, ds(i * CW + 2 * p * CW, CW)]])

            sp.dma_start(vec[0:KT_D, :], a["n_ffn1_pre"].rearrange("o (k p) -> (o k) p", p=P)).then_inc(sem("gain_in"), 16)
            load_gu(0)
            load_down(0)
            with sp.Fori(0, 2) as i:
                for j in range(2 * U_D):
                    load(at(UB["mem"], i, 2 * U_D, j), j, [w_kv[j % U_D][:, :, ds(i * CW + j // U_D * XA_W, CW)]])
            with sp.Fori(0, NG) as g:
                for j in range(4 * U_D):
                    cols = [[(IN_DQ, 256), (IN_DK, 256)], [(IN_DV, 256), (IN_DZ, 256)],
                            [(IN_GQ, 128), (IN_GK, 128), (IN_GV, 256)], [(IN_GR, 256), (IN_XQ, 256)]][j // U_D]
                    load(at(UB["proj"], g, 4 * U_D, j), j,
                         [w_in[j % U_D][:, :, ds(g * w + o, w)] for o, w in cols])
            load_gates(0)
            load_up(0)
            load_gates(1)
            load_up(1)
            with sp.Fori(0, 4) as i:
                for j in range(U_D):
                    load(at(UB["out"], i, U_D, j), j, [w_o[j][:, :, ds(i * CW, CW)]])
            load_gu(1)
            load_down(1)
            for c in range(4):
                sp.wait_ge(sem("h_ready"), 8 + c + 1)
                sp.dma_start(out_v[:, :, c * CW:(c + 1) * CW], nat[:, :, c * CW:(c + 1) * CW]).then_inc(sem("out_stored"), 16)
            sp.wait_ge(sem("out_stored"), 4 * 16)

        @block.gpsimd
        def _(pl):
            made = [0]

            def const(ins):
                ins.then_inc(sem("consts"), 1)
                made[0] += 1
                pl.wait_ge(sem("consts"), made[0])

            def select(t, op, fill, base, pattern, mult):
                const(pl.affine_select(out=t, in_=t, compare_op=op, fill=fill, base=base,
                                       pattern=pattern, channel_multiplier=mult))

            const(pl.memset(ident, 0.0))
            select(ident, ALU.not_equal, 1.0, 0, [[-1, P]], 1)
            const(pl.memset(halfn[:, :], -0.5))
            const(pl.memset(cst[:, 0:1], EPS))
            const(pl.memset(cst[:, 1:2], LOG_SCALE))
            pl.memset(ones[:, :], 1.0).then_inc(sem("first_consts"), 1)
            rows = lambda v: v.rearrange("o (k p) -> (o k) p", p=P)
            for k, name in enumerate(("n_mix_pre", "mem_norm", "n_ffn2_pre"), 1):
                pl.dma_start(vec[k * KT_D:(k + 1) * KT_D, :], rows(a[name])).then_inc(sem("vecs_in"), 16)
            pl.dma_start(vec[4 * KT_D:4 * KT_D + 4, :], rows(a["gla_b_lr"])).then_inc(sem("vecs_in"), 16)
            pl.dma_start(convn[:, :], a["gdn_conv"][0].rearrange("s (k p) -> (s k) p", p=P)).then_inc(sem("vecs_in"), 16)
            const(pl.memset(tri[:, :], 1.0))
            select(tri[:, :], ALU.is_ge, 0.0, 0, [[1, P]], -1)
            const(pl.memset(lowA[:, :], 0.0))
            select(lowA[:, :], ALU.is_ge, NEG, 0, [[1, P]], -1)
            const(pl.memset(highB[:, :], 0.0))
            select(highB[:, :], ALU.is_gt, -NEG, 0, [[-1, P]], 1)
            const(pl.memset(lev[:, :, :], 0.0))
            for l in range(7):
                m = 1 << l
                upper = lev[:, l, :].rearrange("p (b h m) -> p b h m", h=2, m=m)[:, :, 1, :]
                nb = P // (2 * m)
                const(pl.memset(upper, 1.0))
                select(upper, ALU.is_ge, 0.0, 0, [[-2 * m, nb], [0, m]], 1)
                select(upper, ALU.is_ge, 0.0, m - 1, [[2 * m, nb], [0, m]], -1)
            pl.engine_nop().then_inc(sem("all_consts"), 1)
            for name in ("gdn_lo", "gla_lo", "xa_lo"):
                pl.engine_nop().then_inc(sem(name), 1)
            for dst, src in ((gnorm[:, :], a["gla_norm"].broadcast_to([P, GLA_DV])),
                             (dnorm[:, :], a["gdn_norm"].broadcast_to([P, GDN_D])),
                             (alog[:, :], a["gdn_a_log"].broadcast_to([P, GDN_H])),
                             (dtb[:, :], a["gdn_dt_bias"].broadcast_to([P, GDN_H]))):
                pl.dma_start(dst, src).then_inc(sem("small_in"), 16)

            def rsqrt(k, half=False):
                pl.wait_ge(sem("norm_sum"), k + 1)
                f = 4.0 if half else 1.0
                pl.tensor_scalar(rsw[:, k, :], ssum[:, k, :], f / D, f * EPS, ALU.mult, ALU.add).then_inc(sem("norm_mean"), 1)
                pl.wait_ge(sem("norm_mean"), k + 1)
                pl.tensor_tensor(rs[:, k, :], rsw[:, k, :], halfn[:, :], ALU.pow).then_inc(sem("norm_rs"), 1)

            def store_h(b, c):
                pl.wait_ge(sem("h_ready"), 4 * b + c + 1)
                pl.dma_start(h_v[:, :, c * CW:(c + 1) * CW], nat[:, :, c * CW:(c + 1) * CW]).then_inc(sem("h_stored"), 16)

            def fetch(c):
                if c == 0:
                    pl.wait_ge(unit_used, UB["mem"])
                if c >= 2:
                    pl.wait_ge(sem("h_ready"), c - 1)
                pl.dma_start(res[:, c % 2], x_v[:, :, c * CW:(c + 1) * CW]).then_inc(sem(f"res_in{c % 2}"), 16)
                pl.dma_start(post_a[:, c % 2], a["n_ffn1_post"][:, c * CW:(c + 1) * CW].broadcast_to([P, CW])).then_inc(sem(f"res_in{c % 2}"), 16)

            def fetch_block(b, post):
                pl.dma_start(block_post[b][:, :], post.broadcast_to([P, D])).then_inc(sem("post_in"), 16)
                pl.wait_ge(sem("h_stored"), 4 * b * 16)
                pl.dma_start(block_res[b][:, :, :], h_v).then_inc(sem("h_in"), 16)

            rsqrt(R_X)
            for c in range(4):
                if c >= 2:
                    pl.wait_ge(t_done, T_MEM + c - 1)
                    pl.wait_ge(sem("squared"), 8 * R_MEM + 2 * (c - 1))
                pl.dma_start(res[:, c % 2], mem_v[:, :, c * CW:(c + 1) * CW]).then_inc(sem(f"mem_in{c % 2}"), 16)
            rsqrt(R_MEM)
            pl.wait_ge(t_done, T_MEM + 4)
            fetch(0)
            fetch(1)
            rsqrt(R_D1, True)
            for c in range(4):
                store_h(0, c)
                if c + 2 < 4:
                    fetch(c + 2)
            rsqrt(R_H1)
            pl.wait_ge(unit_used, UB["mem"])
            w_all = a["w_in"][0].rearrange("(k p) n -> p k n", p=P)
            pl.dma_start(wsm[:, :, 0:RANK], w_all[:, :, IN_LR:IN_LR + RANK]).then_inc(sem("wsm_in"), 16)
            pl.dma_start(wsm[:, :, RANK:32], w_all[:, :, IN_B:IN_B + 2 * GDN_H]).then_inc(sem("wsm_in"), 16)
            for i in range(2):
                pl.wait_ge(sem("mk_ready"), i + 1)
                pl.dma_start(mk_v[:, 4 * i:4 * i + 4, :], mkT[:, :, :]).then_inc(sem("mk_stored"), 16)
                pl.wait_ge(acc_out[1], QB["mem"] // 2 + i + 1)
                pl.dma_start(mv_v[:, :, i * CW:(i + 1) * CW], mvn[:, :, :]).then_inc(sem("mv_stored"), 16)
            pl.wait_ge(sem("mk_stored"), 2 * 16)
            pl.wait_ge(sem("mv_stored"), 2 * 16)
            pl.wait_ge(unit_used, UB["proj"])
            with pl.Fori(0, NG) as g:
                groups_done(pl, g)
                pl.dma_start(mkh[:, :, :], mk_v[:, ds(g * 2, 2), :]).then_inc(sem("mkv_in"), 16)
                pl.dma_start(mvh[:, :, :], mv_v[:, :, ds(g * 256, 256)]).then_inc(sem("mkv_in"), 16)
                pl.dma_start(lr2g[:, :], a["gla_w_lr2"][0][:, ds(g * P, P)]).then_inc(sem("mkv_in"), 16)
                pl.memset(att[:, :, :, :], 0.0).then_inc(sem("att_zero"), 1)
                pl.wait_ge(sem("group_consts"), g * 3 + 3)
                pl.tensor_tensor(zb[:, :, :].rearrange("p (h t) n -> p h t n", t=NT),
                                 tri[:, :].unsqueeze(1).unsqueeze(1).broadcast_to([P, 2, NT, P]),
                                 gs[:, 0:NT, :].rearrange("p t h -> p h t").unsqueeze(3).broadcast_to([P, 2, NT, P]),
                                 ALU.mult).then_inc(sem("grhs_ready"), 1)
                pl.wait_ge(sem("silu_zr"), g + 1)
                zg4 = zg[:, :, :].rearrange("p t (h n) -> p (t h) n", h=2)
                pl.tensor_tensor(zg4, zg4, dnorm[:, :].unsqueeze(1).broadcast_to([P, 4, P]), ALU.mult).then_inc(sem("zg_ready"), 1)
                pl.tensor_tensor(rg[:, :, :], rg[:, :, :], gnorm[:, :].unsqueeze(1).broadcast_to([P, NT, 256]),
                                 ALU.mult).then_inc(sem("rg_ready"), 1)
            pl.wait_ge(unit_used, UB["up1"])
            fetch_block(1, a["n_mix_post"])
            rsqrt(R_OUT)
            for c in range(4):
                store_h(1, c)
            rsqrt(R_H2)
            pl.wait_ge(unit_used, UB["down2"])
            fetch_block(2, a["n_ffn2_post"])
            rsqrt(R_D2, True)

        @block.tensor
        def _(pe):
            def unit(n, j, hi, lo, k0, par, first, last, before):
                s = j % RING
                pe.wait_ge(lo_ready, n + 1)
                if first and (not isinstance(before, int) or before > 0):
                    pe.wait_ge(acc_out[par], before)
                for k in range(UK):
                    for t in range(NT):
                        cols = slice(t * P, (t + 1) * P)
                        for m, (x, w) in enumerate(((hi, whi), (hi, wlo), (lo, whi))):
                            ins = nc.tensor.matmul(acc[:, par, t, :], x[:, k0 + k, cols], w[:, s, k, :],
                                                   start=first and k == 0 and m == 0,
                                                   stop=last and k == UK - 1 and m == 2)
                ins.then_inc(unit_used, 1)

            def chunk(n0, j0, count, hi, lo, par, before, between=None):
                for j in range(count):
                    unit(n0 + j, j0 + j, hi, lo, UK * j, par, j == 0, j == count - 1, before)
                    if between is not None:
                        between(j0 + j)

            def transposed(tq, src, pair, free=0):
                if not isinstance(tq, int) or tq - free > 0:
                    pe.wait_ge(t_lo, half_tiles(tq - free))
                v = mix[:, 2 * pair:2 * pair + 2, :].rearrange("p b (k s) -> p (b k) s", s=SEQ)
                for blk in range(4):
                    for t in range(NT):
                        ins = nc.tensor.transpose(v[:, blk, t * P:(t + 1) * P], src[:, t, blk * P:(blk + 1) * P], ident)
                ins.then_inc(t_done, 1)

            def gu(f, i, first):
                base, q = UB[f"gu{f + 1}"], QB[f"gu{f + 1}"] // 2

                def between(j):
                    if j == 2 and not first:
                        pe.wait_ge(acc_out[1], q + i)
                        transposed((T_ACT1, T_ACT2)[f] - 1 + i, nat[:, :, CW:2 * CW], 0)
                    if first and j in (0, 2):
                        norm_chunk(f, 2 + j // 2)
                    if first and j < U_D - 1:
                        pe.wait_ge(t_lo, half_tiles((T_X, T_H2)[f]) + j + 2)
                    if first and f == 0 and j == U_D:
                        pe.wait_ge(sem("vecs_in"), 5 * 16)
                        nc.tensor.transpose(mix[:, 3, 0:4 * KT_D + 4], vec[:, :], ident[0:4 * KT_D + 4, 0:4 * KT_D + 4])
                        nc.tensor.transpose(mix[:, 3, P:P + TAPS * 24], convn[:, :],
                                            ident[0:TAPS * 24, 0:TAPS * 24]).then_inc(sem("vecT_done"), 1)

                for half in range(2):
                    chunk(at(base, i, 2 * U_D, half * U_D), half * U_D, U_D, x_hi, x_lo, half, q + i, between)

            def norm_chunk(f, c):
                if f == 0:
                    pe.wait_ge(sem(f"x_in{c}"), 16)
                else:
                    pe.wait_ge(sem("h_ready"), 4 + c + 1)
                transposed((T_X, T_H2)[f] + c, nat[:, :, c * CW:(c + 1) * CW], c % 2, min(c, 1))

            def down(f):
                base, q = UB[f"down{f + 1}"], QB[f"down{f + 1}"] // 2

                def between(j):
                    if j == 2 and i == 0:
                        pe.wait_ge(acc_out[1], q)
                        transposed((T_ACT1, T_ACT2)[f] + N_GU - 1, nat[:, :, CW:2 * CW], 0)
                    if f == 0 and i == 0 and j in (3, 8, 13, 18):
                        c = (j - 3) // 5
                        pe.wait_ge(sem(f"mem_in{c % 2}"), 16 * (c // 2 + 1))
                        transposed(T_MEM + c, res[:, c % 2], c % 2)
                    if i == 0 and j == U_F - 3:
                        pe.wait_ge(t_lo, half_tiles((T_ACT1, T_ACT2)[f] + N_GU))

                for i in range(2):
                    for half in range(2):
                        chunk(at(base, i, 2 * U_F, half * U_F), half * U_F, U_F, act_hi, act_lo, half, q + i, between)

            def memory():
                base, q = UB["mem"], QB["mem"] // 2

                def between(j):
                    j += 2 * U_D * i
                    if j in (3, 5, 7, 9):
                        c = (j - 3) // 2
                        pe.wait_ge(sem("h_ready"), c + 1)
                        transposed(T_U + c, nat[:, :, c * CW:(c + 1) * CW], c % 2, min(c, 1))
                    if j in (12, 25):
                        pe.wait_ge(acc_out[0], q + j // 16 + 1)
                        pe.wait_ge(t_lo, half_tiles(T_U + 4))
                        if j == 25:
                            pe.wait_ge(sem("mk_ready"), 1)
                        v = mix[:, 2:4, :].rearrange("p b (k s) -> p (b k) s", s=SEQ)
                        for blk in range(4):
                            for t in range(NT):
                                ins = nc.tensor.transpose(v[:, blk, t * P:(t + 1) * P], mkn[:, t, blk * P:(blk + 1) * P], ident)
                        ins.then_inc(sem("mk_done"), 1)

                for i in range(2):
                    for half in range(2):
                        chunk(at(base, i, 2 * U_D, half * U_D), half * U_D, U_D, x_hi, x_lo, half, q + i, between)

            def small_steps(j):
                if j == 0:
                    pe.wait_ge(sem("wsm_lo"), 1)
                    for k in range(KT_D):
                        for m, (x, w) in enumerate(((u_hi, wsmh), (u_hi, wsml), (u_lo, wsmh))):
                            ins = nc.tensor.matmul(mix[0:32, 0, 0:SEQ], w[:, k, :], x[:, k, :],
                                                   start=k == 0 and m == 0, stop=k == KT_D - 1 and m == 2)
                    ins.then_inc(sem("small_done"), 1)
                if j == 1:
                    pe.wait_ge(sem("small_T_ready"), 1)
                    for t in range(NT):
                        ins = nc.tensor.transpose(mix[:, 1, t * 32:(t + 1) * 32], small_T[:, t * P:(t + 1) * P], ident[0:32, 0:32])
                    ins.then_inc(sem("small_rows"), 1)
                if j == 3:
                    pe.wait_ge(sem("small_out"), 1)
                    for t in range(NT):
                        ins = nc.tensor.transpose(mix[0:RANK, 1, t * P:(t + 1) * P], small[:, t, 0:RANK], ident)
                    ins.then_inc(sem("lrT_done"), 1)
                if j == 7:
                    pe.wait_ge(sem("logdecay"), 1)
                    av = st[:, 0].rearrange("p t h -> p (t h)")
                    nc.tensor.matmul(mix[:, 2, 0:16], tri[:, :], av, start=True, stop=True)
                    nc.tensor.matmul(mix[:, 2, 16:32], ones[:, :], av, start=True, stop=True).then_inc(sem("gsum_done"), 1)

            def mixer_steps(slot, g):
                j = STEP_AT[slot]
                if j is None:
                    return
                qp = QB["proj"] // 2
                need = lambda name, n=None: pe.wait_ge(sem(name), g + 1 if n is None else n)
                if j == 0:
                    groups_done(pe, g)
                    pe.wait_ge(acc_out[0], qp + g * 2 + 1)
                    pe.wait_ge(acc_out[1], qp + g * 2 + 1)
                    for b in range(3):
                        for h in range(2):
                            for t in range(NT):
                                o = (b % 2) * 256 + h * P
                                ins = nc.tensor.transpose(mix[:, b, h * SEQ + t * P:h * SEQ + (t + 1) * P],
                                                          pr[:, b // 2, t, o:o + P], ident)
                    ins.then_inc(sem("gdn_in"), 1)
                if j == 1:
                    need("grhs_ready")
                    nc.tensor.matmul(mix[:, 3, :], ones[:, :], zb[:, :, :].rearrange("p u n -> p (u n)"),
                                     start=True, stop=True).then_inc(sem("gsums_done"), 1)
                if j == 2:
                    need("qexp_ready")
                    need("dexp_ready")
                    pe.wait_ge(acc_out[1], qp + g * 2 + 2)
                    for b in range(2):
                        for t in range(NT):
                            ins = nc.tensor.transpose(m2(3)[:, b, t * P:(t + 1) * P],
                                                      pr[:, 3, t, 256 + b * P:256 + (b + 1) * P], ident)
                    ins.then_inc(sem("xa_in"), 1)
                if j == 3:
                    need("xq_ready")
                    pe.wait_ge(sem("mkv_in"), g * 48 + 48)
                    for t in range(NT):
                        for b in range(2):
                            ins = nc.tensor.matmul(m2(3)[:, t, :], xqT[:, b, t * P:(t + 1) * P], mkh[:, b, :],
                                                   start=b == 0, stop=b == 1)
                    ins.then_inc(sem("xa_scores"), 1)
                if j == 4:
                    need("sq_ready")
                    for b in range(2):
                        nc.tensor.matmul(mix[:, b, :], ones[:, :], sq[:, 4 * b:4 * b + 4, :].rearrange("p u n -> p (u n)"),
                                         start=True, stop=True)
                    for h in range(2):
                        for t in range(NT):
                            ins = nc.tensor.transpose(m4(2)[:, 2 * h + t, :], conv[:, 4 + h, t * P:(t + 1) * P], ident)
                    ins.then_inc(sem("ssq_done"), 1)
                if j == 6:
                    need("vb_ready")
                    for h in range(2):
                        for t in range(NT):
                            u, cols = 2 * h + t, slice(t * P, (t + 1) * P)
                            kt, qt = conv[:, 2 + h, cols], conv[:, h, cols]
                            nc.tensor.matmul(m4(2)[:, u, :], kt, kt, start=True, stop=True)
                            nc.tensor.matmul(m4(0)[:, u, :], kt, qt, start=True, stop=True)
                            ins = nc.tensor.transpose(m4(1)[:, u, :], kt, ident)
                    ins.then_inc(sem("kk_done"), 1)
                    need("prob_ready")
                    for mt in range(2):
                        for t in range(NT):
                            ins = nc.tensor.transpose(m2(3)[:, mt, t * P:(t + 1) * P], prob[:, t, mt * P:(mt + 1) * P], ident)
                    ins.then_inc(sem("xa_pT"), 1)
                if j == 7:
                    need("l_ready")
                    for u in range(4):
                        ins = nc.tensor.transpose(m4(0)[:, u, :], lmat[:, u, :], ident)
                    ins.then_inc(sem("ux_done"), 1)
                    need("probT_ready")
                    for b in range(2):
                        for mt in range(2):
                            ins = nc.tensor.matmul(m2(3)[:, b, :], mvh[:, mt, b * P:(b + 1) * P], probT[:, mt, :],
                                                   start=mt == 0, stop=mt == 1)
                    ins.then_inc(sem("xa_o"), 1)
                if j == 8:
                    need("kb_ready")
                    need("z_ready", g * 7 + 1)
                    for u in range(4):
                        ins = nc.tensor.transpose(m4(1)[:, u, :], zb[:, u, :], ident)
                    ins.then_inc(sem("xz_done"), 1)
                for l in range(1, 7):
                    if j == 7 + 2 * l:
                        need("xt_ready", g * 7 + l)
                        for u in range(4):
                            ins = nc.tensor.matmul(m4(0)[:, u, :], lmat[:, u, :], xinv[:, u, :], start=True, stop=True)
                        ins.then_inc(sem("ux_done"), 1)
                        if l > 1:
                            for u in range(4):
                                ins = nc.tensor.transpose(m4(2)[:, u, :], xinv[:, u, :], ident)
                            ins.then_inc(sem("x_transposed"), 1)
                    if j == 8 + 2 * l:
                        need("z_ready", g * 7 + l + 1)
                        if l > 1:
                            need("tinv_ready", g * 5 + l - 1)
                        for u in range(4):
                            ins = nc.tensor.matmul(m4(1)[:, u, :], tinv[:, u, :], zb[:, u, :], start=True, stop=True)
                        ins.then_inc(sem("xz_done"), 1)
                if j == 9:
                    need("xa_lo", g + 2)
                    pe.wait_ge(acc_out[0], qp + g * 2 + 2)
                    for b in range(2):
                        for t in range(NT):
                            ins = nc.tensor.transpose(m2(3)[:, b, t * P:(t + 1) * P], pr[:, 2, t, b * P:(b + 1) * P], ident)
                    ins.then_inc(sem("gla_in"), 1)
                if j == 10:
                    need("gqk_ready")
                    nc.tensor.matmul(mix[:, 3, 0:SEQ], lr2g[:, :], lrT[:, :], start=True, stop=True).then_inc(sem("gla_lr"), 1)
                for n in range(4):
                    if j == 13 + 2 * n:
                        need("gqe_ready", g * 4 + n + 1)
                        if n:
                            need("att_ready", g * 4 + n)
                        for li in range(2):
                            for t in range(NT):
                                cols = slice(t * P, (t + 1) * P)
                                k_, q_ = (ge[:, li, cols], gq[:, li, cols]) if n or li else (gqk[:, 1, cols], gqk[:, 0, cols])
                                ins = nc.tensor.matmul(m4(3)[:, 2 * li + t, :], k_, q_, start=True, stop=True)
                        ins.then_inc(sem("gla_s"), 1)
                if j == 21:
                    need("gx_ready")
                    need("att_ready", g * 4 + 4)
                    nc.tensor.matmul(mix[:, 3, 0:P], gq[:, 0, P:2 * P], gq[:, 0, 0:P], start=True, stop=True).then_inc(sem("gla_x"), 1)
                if j == 21:
                    need("xt_ready", g * 7 + 7)
                    for h in range(2):
                        nc.tensor.matmul(m4(0)[:, h, :], xinv[:, 2 * h, :], vb[:, 2 * h, :], start=True, stop=True)
                        ins = nc.tensor.matmul(m4(2)[:, h, :], kbn[:, h, :], xinv[:, 2 * h + 1, :], start=True, stop=True)
                    ins.then_inc(sem("gdn_uw"), 1)
                if j == 22:
                    need("vn_ready", g * 2 + 1)
                    for h in range(2):
                        ins = nc.tensor.matmul(m4(1)[:, h, :], kend[:, h, :], vnew[:, 2 * h, :], start=True, stop=True)
                    ins.then_inc(sem("gdn_s"), 1)
                    need("attx_ready")
                    need("att_sum")
                    v = pr[:, 2, :, 256:512]
                    nc.tensor.matmul(m2(3)[:, 0, :], att[:, 0, 0, :], v[:, 0], start=True, stop=True)
                    nc.tensor.matmul(m2(3)[:, 1, :], att[:, 0, 1, :], v[:, 1], start=True, stop=False)
                    nc.tensor.matmul(m2(3)[:, 1, :], attx[:, :], v[:, 0], start=False, stop=True).then_inc(sem("gla_o"), 1)
                if j == 23:
                    need("wT_ready")
                    need("state_ready")
                    for h in range(2):
                        nc.tensor.matmul(m4(0)[:, h, :], xinv[:, 2 * h + 1, :], vb[:, 2 * h + 1, :], start=True, stop=False)
                        ins = nc.tensor.matmul(m4(0)[:, h, :], wTn[:, h, :], state[:, h, :], start=False, stop=True)
                    ins.then_inc(sem("gdn_v1"), 1)
                if j == 24:
                    need("vn_ready", g * 2 + 2)
                    for h in range(2):
                        nc.tensor.matmul(m4(2)[:, 2 * h, :], attnT[:, 2 * h, :], vnew[:, 2 * h, :], start=True, stop=True)
                        nc.tensor.matmul(m4(2)[:, 2 * h + 1, :], attnT[:, 2 * h + 1, :], vnew[:, 2 * h + 1, :], start=True, stop=False)
                        ins = nc.tensor.matmul(m4(2)[:, 2 * h + 1, :], qe[:, h, :], state[:, h, :], start=False, stop=True)
                    ins.then_inc(sem("gdn_o"), 1)
                if j == 26:
                    need("ggo_ready")
                    for b in range(2):
                        for t in range(NT):
                            ins = nc.tensor.transpose(m2(3)[:, b, t * P:(t + 1) * P], ggo[:, t, b * P:(b + 1) * P], ident)
                    ins.then_inc(sem("gla_oT"), 1)
                if j == 27:
                    need("og_ready")
                    for h in range(2):
                        for t in range(NT):
                            ins = nc.tensor.transpose(m2(0)[:, h, t * P:(t + 1) * P], og[:, 2 * h + t, :], ident)
                    ins.then_inc(sem("gdn_oT"), 1)

            def group(g, mixed):
                for c in range(4):
                    chunk(at(UB["proj"], g, 4 * U_D, c * U_D), c * U_D, U_D, u_hi, u_lo, c % 2,
                          QB["proj"] // 2 + g * 2 + c // 2, (lambda j: mixer_steps(j, mixed)) if mixed is not None else small_steps)

            def gate_logits(p, mixed):
                for k in range(6):
                    chunk(at(UB[f"gates{p}"], 0, 0, k * U_D), k * U_D, U_D, u_hi, u_lo, k % 2, QB[f"gates{p}"] // 2 + k // 2,
                          (lambda j: mixer_steps(j, mixed)) if mixed is not None else
                          (lambda j: mixture(2 * p - 1) if j == 1 else None))

            def mixture(n):
                pe.wait_ge(sem("m_ready"), n + 1)
                transposed(T_M + n, msum[:, :, :], 0)

            def up(p):
                groups_done(pe, NG)
                for n2 in range(2):
                    for br in range(3):
                        k = 3 * n2 + br
                        chunk(UB[f"up{p}"] + k * U_O, k * U_O, U_O, o_hi[:, br], o_lo[:, br], k % 2,
                              QB[f"up{p}"] // 2 + k // 2, lambda j: mixture(2 * p) if j == 13 else None)

            def output():
                def between(j):
                    if j == 1:
                        mixture(3)
                    if j == 5:
                        pe.wait_ge(t_lo, half_tiles(T_M + 4))
                pe.wait_ge(t_lo, half_tiles(T_M + 3))
                for c in range(4):
                    chunk(UB["out"] + c * U_D, c * U_D, U_D, x_hi, x_lo, c % 2, QB["out"] // 2 + c // 2, between)

            pe.wait_ge(sem("first_consts"), 1)
            pe.wait_ge(sem("gain_in"), 16)
            nc.tensor.transpose(mix[:, 3, 0:KT_D], vec[0:KT_D, :], ident[0:KT_D, 0:KT_D]).then_inc(sem("vecT_done"), 1)
            norm_chunk(0, 0)
            pe.wait_ge(sem("vecT_ready"), 1)
            norm_chunk(0, 1)
            pe.wait_ge(t_lo, half_tiles(T_X) + 1)
            gu(0, 0, True)
            with pe.Fori(1, N_GU) as i:
                gu(0, i, False)
            down(0)
            memory()
            pe.wait_ge(t_lo, half_tiles(T_U + 4))
            pe.wait_ge(sem("all_consts"), 1)
            group(0, None)
            with pe.Fori(1, NG) as g:
                group(g, g - 1)
            gate_logits(0, NG - 1)
            up(0)
            gate_logits(1, None)
            up(1)
            output()
            norm_chunk(1, 0)
            norm_chunk(1, 1)
            pe.wait_ge(t_lo, half_tiles(T_H2) + 1)
            gu(1, 0, True)
            with pe.Fori(1, N_GU) as i:
                gu(1, i, False)
            down(1)

        @block.scalar
        def _(ac):
            act = nc.scalar.activation

            def split(n, per_i, j):
                s = j % RING
                i, n0, per = per_i
                slot_loads = (n0 + LOOK) // RING + j // RING + 1
                ac.wait_ge(raw_full[s], i * (per // RING * LOADED) + LOADED * slot_loads)
                ac.wait_ge(unit_used, n + 1)
                act(whi[:, s], raw[:, s], ACT.Copy).then_inc(hi_ready, 1)

            def slots(n0, i, per, tasks, until=None):
                for j in range(per):
                    if until is None or j + LOOK < until:
                        split(at(n0, i, per, j), (i, n0, per), j)
                    tasks(j)

            def squares(k, c, src):
                for t in range(NT):
                    n = 8 * k + 2 * c + t
                    if n:
                        ac.wait_ge(sem("squared"), n)
                    act(junk[:, :], src[:, t, :], ACT.Square, accum_out=ssp[:, k, t, c:c + 1]).then_inc(sem("squared"), 1)

            def square_product(n, par, b, c):
                k = (None, R_OUT, R_D2)[b]
                ac.wait_ge(unit_used, n + 1)
                for t in range(NT):
                    ac.wait_ge(sem("squared"), 8 * k + 2 * c + t)
                    if t == 1:
                        ac.wait_ge(sem("taken"), 8 * (b - 1) + 2 * c + 1)
                    act(junk[:, :], acc[:, par, t, :], ACT.Square, accum_out=ssp[:, k, t, c:c + 1]).then_inc(sem("squared"), 1)

            def upper(tq, dst, pair, gain=None, scale=1.0):
                v = mix[:, 2 * pair:2 * pair + 2, :].rearrange("p b (k s) -> p (b k) s", s=SEQ)
                ac.wait_ge(t_done, tq + 1)
                if gain is None:
                    act(dst, v, ACT.Copy, scale=scale).then_inc(t_hi, 2)
                else:
                    for half in range(2):
                        for blk in (2 * half, 2 * half + 1):
                            ins = act(dst[:, blk, :], v[:, blk, :], ACT.Copy, scale=vecT[:, gain + blk:gain + blk + 1])
                        ins.then_inc(t_hi, 1)

            def take_out(n, par, dst, k):
                ac.wait_ge(unit_used, n + 1)
                for t in range(NT):
                    ins = act(dst[:, t, :], acc[:, par, t, :], ACT.Copy, scale=rs[:, k, t:t + 1])
                ins.then_inc(acc_out[par], 1)

            def gu(f, i, first):
                n0, q = UB[f"gu{f + 1}"], QB[f"gu{f + 1}"] // 2

                def tasks(j):
                    if first and j in (0, 2):
                        first_upper(f, 2 + j // 2)
                    if first and 3 <= j < 7:
                        c = j - 3
                        squares((R_X, R_H2)[f], c, nat[:, :, c * CW:(c + 1) * CW])
                    if first and f == 0 and j == U_D:
                        ac.wait_ge(sem("vecT_done"), 2)
                        act(vecT[:, KT_D:], mix[:, 3, KT_D:4 * KT_D + 4], ACT.Copy).then_inc(sem("vecT_ready"), 1)
                        act(convT[:, :, :, :].rearrange("p a b c -> p (a b c)"), mix[:, 3, P:P + TAPS * 24],
                            ACT.Copy).then_inc(sem("vecT_ready"), 1)
                        ac.wait_ge(sem("vecT_ready"), 3)
                    if j == 2 and not first:
                        upper((T_ACT1, T_ACT2)[f] - 1 + i, act_hi[:, ds(i * 4 - 4, 4), :], 0)
                    if j == U_D - 1:
                        if first:
                            ac.wait_ge(sem("norm_rs"), (R_X, R_H2)[f] + 1)
                            ac.wait_ge(t_lo, half_tiles((T_X, T_H2)[f] + 4))
                            if f == 1:
                                ac.wait_ge(sem("h_stored"), 8 * 16)
                        ac.wait_ge(unit_used, at(n0, i, 2 * U_D, j) + 1)
                        if not first:
                            ac.wait_ge(acc_out[1], q + i)
                        for t in range(NT):
                            ins = act(nat[:, t, 0:CW], acc[:, 0, t, :], ACT.Silu, scale=rs[:, (R_X, R_H2)[f], t:t + 1])
                        ins.then_inc(acc_out[0], 1)

                slots(n0, i, 2 * U_D, tasks)

            def first_upper(f, c):
                upper((T_X, T_H2)[f] + c, x_hi[:, 4 * c:4 * c + 4, :], c % 2, (0, 3 * KT_D)[f] + 4 * c)

            def down(f):
                n0, q = UB[f"down{f + 1}"], QB[f"down{f + 1}"] // 2

                def tasks(j):
                    if j == 2 and i == 0:
                        upper((T_ACT1, T_ACT2)[f] + N_GU - 1, act_hi[:, KT_F - 4:KT_F, :], 0)
                    if f == 0 and i == 0 and j in (3, 8, 13, 18):
                        c = (j - 3) // 5
                        ac.wait_ge(unit_used, UB["down1"])
                        upper(T_MEM + c, x_hi[:, 4 * c:4 * c + 4, :], c % 2, 2 * KT_D + 4 * c)
                        squares(R_MEM, c, res[:, c % 2])
                    if j % U_F == U_F - 1:
                        par = j // U_F
                        c = 2 * i + par
                        if f == 0:
                            ac.wait_ge(acc_out[par], q + i + 1)
                            squares(R_D1, c, nat[:, :, c * CW:(c + 1) * CW])
                        else:
                            square_product(at(n0, i, 2 * U_F, j), par, 2, c)

                for i in range(2):
                    slots(n0, i, 2 * U_F, tasks, until=2 * U_F if (f, i) == (1, 1) else None)

            def memory():
                def tasks(j):
                    if j in (3, 5, 7, 9):
                        c = (j - 3) // 2
                        ac.wait_ge(unit_used, UB["mem"])
                        upper(T_U + c, u_hi[:, 4 * c:4 * c + 4, :], c % 2, KT_D + 4 * c)
                    if j in (4, 6, 8, 10):
                        c = (j - 4) // 2
                        squares(R_H1, c, nat[:, :, c * CW:(c + 1) * CW])
                    if j == SPLIT_SMALL:
                        ac.wait_ge(sem("small_in"), 4 * 16)
                        ac.wait_ge(sem("wsm_in"), 2 * 16)
                        act(wsmh[:, :, :], wsm[:, :, :], ACT.Copy).then_inc(sem("wsm_hi"), 1)
                    if j % U_D == U_D - 1:
                        c = j // U_D
                        if c == 0:
                            ac.wait_ge(sem("norm_rs"), R_MEM + 1)
                        if c == 2:
                            ac.wait_ge(sem("mk_done"), 1)
                        if c == 3:
                            ac.wait_ge(sem("mv_stored"), 16)
                        take_out(UB["mem"] + j, c % 2, (mkn, mvn)[c % 2][:, :, :], R_MEM)
                    if j in (12, 25):
                        ac.wait_ge(sem("mk_done"), 1 + j // 16)
                        if j == 25:
                            ac.wait_ge(sem("mk_stored"), 16)
                        act(mkT[:, :, :], mix[:, 2:4, :].rearrange("p b (k s) -> p (b k) s", s=SEQ), ACT.Copy).then_inc(sem("mk_ready"), 1)
                slots(UB["mem"], 0, 4 * U_D, tasks)

            stc = [0]

            def st_step(ins):
                ins.then_inc(sem("st_act"), 1)
                stc[0] += 1
                ac.wait_ge(sem("st_act"), stc[0])

            def small_steps(j):
                if j == 0:
                    ac.wait_ge(sem("small_done"), 1)
                    act(small_T[:, :], mix[0:32, 0, 0:SEQ], ACT.Copy).then_inc(sem("small_T_ready"), 1)
                if j == 2:
                    ac.wait_ge(sem("norm_rs"), R_H1 + 1)
                    ac.wait_ge(sem("small_rows"), 1)
                    for t in range(NT):
                        ins = act(small[:, t, :], mix[:, 1, t * 32:(t + 1) * 32], ACT.Copy, scale=rs[:, R_H1, t:t + 1])
                    ins.then_inc(sem("small_out"), 1)
                    ac.wait_ge(sem("small_out"), 1)
                    act(stw[:, 0], small[:, :, RANK:RANK + GDN_H], ACT.Tanh, scale=0.5).then_inc(sem("tanh_b"), 1)
                if j == 3:
                    ac.wait_ge(sem("lrT_done"), 1)
                    act(lrT[:, :], mix[0:RANK, 1, 0:SEQ], ACT.Copy).then_inc(sem("lrT_ready"), 1)
                    ac.wait_ge(sem("a_bias"), 1)
                    st_step(act(stw[:, 2], stw[:, 1], ACT.Abs))
                    st_step(act(stw[:, 2], stw[:, 2], ACT.Exp, scale=-1.0))
                    st_step(act(alog[:, :], alog[:, :], ACT.Exp))
                    act(stw[:, 2], stw[:, 2], ACT.Ln, bias=1.0).then_inc(sem("softplus"), 1)
                if j == 8:
                    ac.wait_ge(sem("gsum_done"), 1)
                    act(stw[:, 3].rearrange("p t h -> p (t h)"), mix[:, 2, 0:16], ACT.Exp).then_inc(sem("exp_g"), 1)
                    ac.wait_ge(sem("g_rest"), 1)
                    act(st[:, 4], stw[:, 0], ACT.Exp).then_inc(sem("exp_rest"), 1)

            def mixer_steps(slot, g):
                j = STEP_AT[slot]
                if j is None:
                    return
                need = lambda name, n=None: ac.wait_ge(sem(name), g + 1 if n is None else n)
                qp = QB["proj"] // 2
                if j == 0:
                    groups_done(ac, g)
                    need("gdn_in")
                    need("group_consts", g * 3 + 3)
                    for b in range(3):
                        for h in range(2):
                            ins = act(conv[:, 2 * b + h, :], mix[:, b, h * SEQ:(h + 1) * SEQ], ACT.Copy,
                                      scale=cwg[:, 3 * (TAPS - 1) + b, h:h + 1])
                        ins.then_inc(sem("conv_seed"), 1)
                if j == 1:
                    need("gsums_done")
                    act(qe[:, :, :], mix[:, 3, :].rearrange("p (h t n) -> p h t n", t=NT, n=P)[:, :, 1, :], ACT.Exp).then_inc(sem("qexp_ready"), 1)
                if j == 2:
                    need("dexp_ready")
                    act(decT[:, :, :], decT[:, :, :], ACT.Exp)
                    act(dec[:, :, :], dec[:, :, :], ACT.Exp, scale=-1.0).then_inc(sem("dec_ready"), 1)
                    need("xa_in")
                    act(xqT[:, :, :], m2(3), ACT.Copy).then_inc(sem("xq_ready"), 1)
                    need("conv_done", g * 3 + 1)
                    act(conv[:, 0:2, :], conv[:, 0:2, :], ACT.Silu).then_inc(sem("conv_silu"), 1)
                if j == 3:
                    for b in range(1, 3):
                        need("conv_done", g * 3 + b + 1)
                        act(conv[:, 2 * b:2 * b + 2, :], conv[:, 2 * b:2 * b + 2, :], ACT.Silu).then_inc(sem("conv_silu"), 1)
                    need("conv_silu", g * 3 + 3)
                    act(sq[:, :, :], conv[:, 0:4, :].rearrange("p a (b n) -> p (a b) n", n=P), ACT.Square).then_inc(sem("sq_ready"), 1)
                    act(zg[:, :, :], pr[:, 1, :, 256:512], ACT.Silu)
                    act(rg[:, :, :], pr[:, 3, :, 0:256], ACT.Silu).then_inc(sem("silu_zr"), 1)
                if j == 4:
                    need("ssq_done")
                    act(rn, mix[:, 0:2, :].rearrange("p b n -> p (b n)"), ACT.Ln, bias=cst[:, 0:1]).then_inc(sem("rn_log"), 1)
                    need("rn_log")
                    act(rn[:, 0:CW], rn[:, 0:CW], ACT.Exp, scale=-0.5, bias=cst[:, 1:2])
                    act(rn[:, CW:2 * CW], rn[:, CW:2 * CW], ACT.Exp, scale=-0.5).then_inc(sem("rn_ready"), 1)
                    need("xa_nb")
                    for t in range(NT):
                        ins = act(prob[:, t, :], m2(3)[:, t, :], ACT.Exp, scale=XA_D ** -0.5, bias=mx[:, 1, t:t + 1],
                                  accum_out=mx[:, 2, t:t + 1])
                    ins.then_inc(sem("xa_exp"), 1)
                if j == 6:
                    need("kk_done")
                    for h in range(2):
                        act(kend[:, h, :], m4(1)[:, 2 * h, :], ACT.Copy, scale=gs[:, 8, h:h + 1])
                        ins = act(kbn[:, h, :], m4(1)[:, 2 * h + 1, :], ACT.Copy, scale=gs[:, 7, h:h + 1])
                    ins.then_inc(sem("kb_ready"), 1)
                    need("xa_pT")
                    act(probT[:, :, :], m2(3), ACT.Copy).then_inc(sem("probT_ready"), 1)
                if j == 7:
                    need("xa_o")
                    act(o_hi[:, 2, ds(g * 2, 2), :], m2(3), ACT.Copy).then_inc(sem("xa_hi"), 1)
                if j == 9:
                    need("gla_in")
                    act(gqk[:, 0, :], m2(3)[:, 0, :], ACT.Copy, scale=GLA_DK ** -0.5)
                    act(gqk[:, 1, :], m2(3)[:, 1, :], ACT.Copy).then_inc(sem("gqk_ready"), 1)
                if j == 10:
                    need("gla_lr")
                    act(lsl, mix[:, 3, 0:SEQ], ACT.Abs, bias=blr[:, 0:1]).then_inc(sem("lsl"), 1)
                    need("lsl", g * 2 + 1)
                    act(lsl, lsl, ACT.Exp, scale=-1.0).then_inc(sem("lsl"), 1)
                    need("lsl", g * 2 + 2)
                    act(lsl, lsl, ACT.Ln, bias=1.0).then_inc(sem("lsl_ready"), 1)
                for l in range(2, 7):
                    if j == 7 + 2 * l:
                        need("x_transposed", g * 5 + l - 1)
                        act(tinv, m4(2), ACT.Copy).then_inc(sem("tinv_ready"), 1)
                for n in range(4):
                    if j == 11 + 2 * n:
                        lo = 1 if n == 0 else 0
                        need("gd_ready", g * 4 + n + 1)
                        act(ge[:, lo:2, :], ge[:, lo:2, :], ACT.Abs).then_inc(sem("gabs"), 1)
                        need("gabs", g * 4 + n + 1)
                        act(ge[:, lo:2, :], ge[:, lo:2, :], ACT.Exp, scale=-1.0 / GLA_TAU).then_inc(sem("gexp"), 1)
                if j == 19:
                    need("gla_s", g * 4 + 4)
                    act(bias_c[:, :], cb[:, 0, P - 1:P], ACT.Copy, scale=1.0 / GLA_TAU).then_inc(sem("bias_c"), 1)
                    need("bias_c")
                    act(ge[:, 0, 0:P], cb[:, 1, :], ACT.Exp, scale=1.0 / GLA_TAU)
                    act(ge[:, 0, P:2 * P], cb[:, 0, :], ACT.Exp, scale=-1.0 / GLA_TAU, bias=bias_c[:, 0:1]).then_inc(sem("gxe_ready"), 1)
                if j == 21:
                    need("gla_x")
                    act(attx[:, :], mix[:, 3, 0:P], ACT.Copy).then_inc(sem("attx_ready"), 1)
                    need("gdn_uw")
                    act(wTn, m4(2)[:, 0:2, :], ACT.Copy).then_inc(sem("wT_ready"), 1)
                if j == 22:
                    need("gdn_s")
                    act(state, m4(1)[:, 0:2, :], ACT.Copy).then_inc(sem("state_ready"), 1)
                    need("gla_o")
                    act(gq[:, :, :], m2(3), ACT.Square).then_inc(sem("gsq_ready"), 1)
                if j == 24:
                    need("gss_ready")
                    act(gss[:, :], gss[:, :], ACT.Ln, scale=1.0 / GLA_DV, bias=cst[:, 0:1]).then_inc(sem("gln"), 1)
                    need("gln")
                    act(gss[:, :], gss[:, :], ACT.Exp, scale=-0.5).then_inc(sem("grn_ready"), 1)
                    need("gdn_o")
                    act(osq[:, :, :], m4(2), ACT.Square).then_inc(sem("osq_ready"), 1)
                if j == 25:
                    need("oss_ready")
                    act(oss[:, :], oss[:, :], ACT.Ln, scale=1.0 / GDN_D, bias=cst[:, 0:1]).then_inc(sem("oln"), 1)
                    need("oln")
                    act(oss[:, :], oss[:, :], ACT.Exp, scale=-0.5).then_inc(sem("orn_ready"), 1)
                if j == 26:
                    need("gla_oT")
                    act(o_hi[:, 0, ds(g * 2, 2), :], m2(3), ACT.Copy).then_inc(sem("gla_hi"), 1)
                if j == 27:
                    need("gdn_oT")
                    act(o_hi[:, 1, ds(g * 2, 2), :], m2(0), ACT.Copy).then_inc(sem("gdn_hi"), 1)

            def free_chunk(c, mixed):
                if c < 4:
                    for name in (("gdn_in",), ("gdn_in", "silu_zr"), ("gla_in", "gla_o"), ("xa_in", "silu_zr"))[c]:
                        ac.wait_ge(sem(name), mixed + 1)
                else:
                    groups_done(ac, mixed + 1)

            def group(g, mixed):
                def tasks(j):
                    if mixed is None:
                        small_steps(j)
                    else:
                        mixer_steps(j, mixed)
                    if j in TAKE_AT:
                        c = TAKE_AT.index(j)
                        if mixed is None and c == 0:
                            ac.wait_ge(sem("h_stored"), 4 * 16)
                            ac.wait_ge(t_lo, half_tiles(T_U + 4))
                        elif mixed is not None:
                            free_chunk(c, mixed)
                        take_out(at(UB["proj"], g, 4 * U_D, (c + 1) * U_D - 1), c % 2, pr[:, c], R_H1)
                slots(UB["proj"], g, 4 * U_D, tasks)

            def gate_logits(p, mixed):
                def tasks(j):
                    if mixed is not None:
                        mixer_steps(j, mixed)
                    elif j == 1:
                        mixture(2 * p - 1)
                    if j in TAKE_AT:
                        k = TAKE_AT.index(j)
                        if mixed is not None:
                            free_chunk(k, mixed)
                        elif k == 0:
                            ac.wait_ge(sem("m_ready"), 2 * p)
                        take_out(UB[f"gates{p}"] + (k + 1) * U_D - 1, k % 2, gates[:, k], R_H1)
                slots(UB[f"gates{p}"], 0, 6 * U_D, tasks)

            def mixture(n):
                upper(T_M + n, x_hi[:, 4 * n:4 * n + 4, :], 0, scale=0.5)

            def up(p):
                def tasks(j):
                    if j % U_O == 0:
                        k = j // U_O
                        if k == 0:
                            ac.wait_ge(acc_out[1], QB[f"gates{p}"] // 2 + 3)
                        act(gates[:, k], gates[:, k], ACT.Tanh, scale=0.5).then_inc(sem("gate_ready"), 1)
                    if j == 13:
                        mixture(2 * p)
                slots(UB[f"up{p}"], 0, 6 * U_O, tasks)

            def output():
                def tasks(j):
                    if j == 1:
                        mixture(3)
                    if j % U_D == U_D - 1:
                        c = j // U_D
                        square_product(UB["out"] + j, c % 2, 1, c)
                slots(UB["out"], 0, 4 * U_D, tasks)

            for c in range(4):
                ac.dma_start(nat[:, :, c * CW:(c + 1) * CW], x_v[:, :, c * CW:(c + 1) * CW]).then_inc(sem(f"x_in{c}"), 16)
            ac.wait_ge(sem("first_consts"), 1)
            act(bias_c[:, :], cst[:, 0:1], ACT.Copy).then_inc(sem("tables"), 1)
            ac.wait_ge(sem("vecT_done"), 1)
            act(vecT[:, 0:KT_D], mix[:, 3, 0:KT_D], ACT.Copy).then_inc(sem("vecT_ready"), 1)
            ac.wait_ge(sem("vecT_ready"), 1)
            for s in range(RING):
                if s % 2 == 0:
                    first_upper(0, s // 2)
                ac.wait_ge(raw_full[s], LOADED)
                act(whi[:, s], raw[:, s], ACT.Copy).then_inc(hi_ready, 1)
            gu(0, 0, True)
            with ac.Fori(1, N_GU) as i:
                gu(0, i, False)
            down(0)
            memory()
            group(0, None)
            with ac.Fori(1, NG) as g:
                group(g, g - 1)
            gate_logits(0, NG - 1)
            up(0)
            gate_logits(1, None)
            up(1)
            output()
            first_upper(1, 0)
            first_upper(1, 1)
            gu(1, 0, True)
            with ac.Fori(1, N_GU) as i:
                gu(1, i, False)
            down(1)

        @block.vector
        def _(ve):
            tt, stt, ts = nc.vector.tensor_tensor, nc.vector.scalar_tensor_tensor, nc.vector.tensor_scalar

            def split(n, j):
                s = j % RING
                ve.wait_ge(hi_ready, n + LOOK + 1)
                tt(wlo[:, s], raw[:, s], whi[:, s].bitcast(fp32), ALU.subtract).then_inc(lo_ready, 1)

            def slots(n0, i, per, tasks, until=None):
                for j in range(per):
                    tasks(j)
                    if until is None or j + LOOK < until:
                        split(at(n0, i, per, j), j)

            def lower(tq, dst, dst_hi, pair, gain=None, scale=None):
                v = mix[:, 2 * pair:2 * pair + 2, :].rearrange("p b (k s) -> p (b k) s", s=SEQ)
                hi = dst_hi.bitcast(fp32)
                if gain is not None:
                    for half in range(2):
                        ve.wait_ge(t_hi, half_tiles(tq) + half + 1)
                        for blk in (2 * half, 2 * half + 1):
                            ins = stt(dst[:, blk, :], v[:, blk, :], vecT[:, gain + blk:gain + blk + 1], hi[:, blk, :],
                                      ALU.mult, ALU.subtract)
                        ins.then_inc(t_lo, 1)
                    return
                ve.wait_ge(t_hi, half_tiles(tq + 1))
                if scale is not None:
                    ins = stt(dst, v, scale, hi, ALU.mult, ALU.subtract)
                else:
                    ins = tt(dst, v, hi, ALU.subtract)
                ins.then_inc(t_lo, 2)

            def first_lower(f, c):
                rows = slice(4 * c, 4 * c + 4)
                lower((T_X, T_H2)[f] + c, x_lo[:, rows, :], x_hi[:, rows, :], c % 2, (0, 3 * KT_D)[f] + 4 * c)

            def norm_sum(k):
                ve.wait_ge(sem("squared"), 8 * k + 8)
                nc.vector.tensor_reduce(ssum[:, k, :], ssp[:, k], AXX, ALU.add).then_inc(sem("norm_sum"), 1)

            def residual(b, k, c):
                if c == 0:
                    ve.wait_ge(sem("norm_rs"), k + 1)
                cs = slice(c * CW, (c + 1) * CW)
                if b == 0:
                    ve.wait_ge(sem(f"res_in{c % 2}"), 32 * (c // 2 + 1))
                    for t in range(NT):
                        ins = stt(nat[:, t, cs], nat[:, t, cs], rs[:, k, t:t + 1], post_a[:, c % 2], ALU.mult, ALU.mult)
                    ins.then_inc(sem("normed"), 1)
                    ve.wait_ge(sem("normed"), c + 1)
                    tt(nat[:, :, cs], nat[:, :, cs], res[:, c % 2], ALU.add).then_inc(sem("h_ready"), 1)
                else:
                    if c == 0:
                        ve.wait_ge(sem("h_in"), 16 * b)
                        ve.wait_ge(sem("taken"), 8 * b)
                    for t in range(NT):
                        ins = stt(nat[:, t, cs], nat[:, t, cs], rs[:, k, t:t + 1], block_res[b][:, t, cs], ALU.mult, ALU.add)
                    ins.then_inc(sem("h_ready"), 1)

            def gu(f, i, first):
                n0, q = UB[f"gu{f + 1}"], QB[f"gu{f + 1}"] // 2
                k = (R_X, R_H2)[f]

                def tasks(j):
                    if first and f == 1 and j == 0:
                        residual(1, R_OUT, 3)
                    if first and j in (0, 2):
                        first_lower(f, 2 + j // 2)
                    if first and j == 6:
                        norm_sum(k)
                    if j == 2 and not first:
                        rows = ds(i * 4 - 4, 4)
                        lower((T_ACT1, T_ACT2)[f] - 1 + i, act_lo[:, rows, :], act_hi[:, rows, :], 0)
                    if j == 2 * U_D - 1:
                        if first:
                            ve.wait_ge(sem("norm_rs"), k + 1)
                        ve.wait_ge(unit_used, at(n0, i, 2 * U_D, j) + 1)
                        ve.wait_ge(acc_out[0], q + i + 1)
                        ve.wait_ge(t_done, (T_ACT1, T_ACT2)[f] + i)
                        for t in range(NT):
                            ins = stt(nat[:, t, CW:2 * CW], acc[:, 1, t, :], rs[:, k, t:t + 1], nat[:, t, 0:CW], ALU.mult, ALU.mult)
                        ins.then_inc(acc_out[1], 1)

                slots(n0, i, 2 * U_D, tasks)

            def take_product(n, par, b, c):
                ve.wait_ge(unit_used, n + 1)
                cs = slice(c * CW, (c + 1) * CW)
                if b == 0:
                    nc.vector.tensor_copy(nat[:, :, cs], acc[:, par]).then_inc(acc_out[par], 1)
                    return
                if c == 0:
                    ve.wait_ge(sem("post_in"), 16 * b)
                tt(nat[:, 1, cs], acc[:, par, 1, :], block_post[b][:, cs], ALU.mult).then_inc(sem("taken"), 1)
                ve.wait_ge(sem("squared"), 8 * (None, R_OUT, R_D2)[b] + 2 * c + 1)
                tt(nat[:, 0, cs], acc[:, par, 0, :], block_post[b][:, cs], ALU.mult).then_inc(sem("taken"), 1)
                ve.wait_ge(sem("taken"), 8 * (b - 1) + 2 * c + 2)
                ve.wait_ge(sem("squared"), 8 * (None, R_OUT, R_D2)[b] + 2 * c + 2)
                nc.vector.engine_nop().then_inc(acc_out[par], 1)

            def down(f):
                n0, q = UB[f"down{f + 1}"], QB[f"down{f + 1}"] // 2

                def tasks(j):
                    if j == 2 and i == 0:
                        lower((T_ACT1, T_ACT2)[f] + N_GU - 1, act_lo[:, KT_F - 4:KT_F, :], act_hi[:, KT_F - 4:KT_F, :], 0)
                    if f == 0 and i == 0 and j == 3:
                        ve.wait_ge(sem("vecT_ready"), 3)
                    if f == 0 and i == 0 and j in (3, 8, 13, 18):
                        c = (j - 3) // 5
                        rows = slice(4 * c, 4 * c + 4)
                        lower(T_MEM + c, x_lo[:, rows, :], x_hi[:, rows, :], c % 2, 2 * KT_D + 4 * c)
                    if f == 0 and i == 0 and j == 19:
                        norm_sum(R_MEM)
                    if j % U_F == U_F - 1:
                        take_product(at(n0, i, 2 * U_F, j), j // U_F, 2 * f, 2 * i + j // U_F)

                for i in range(2):
                    slots(n0, i, 2 * U_F, tasks, 2 * U_F if (f, i) == (1, 1) else None)

            def memory():
                def tasks(j):
                    if j == 0:
                        norm_sum(R_D1)
                    if j in (1, 3, 5, 7):
                        residual(0, R_D1, (j - 1) // 2)
                    if j in (3, 5, 7, 9):
                        c = (j - 3) // 2
                        rows = slice(4 * c, 4 * c + 4)
                        lower(T_U + c, u_lo[:, rows, :], u_hi[:, rows, :], c % 2, KT_D + 4 * c)
                    if j == 11:
                        norm_sum(R_H1)
                    if j == SPLIT_SMALL:
                        ve.wait_ge(sem("wsm_hi"), 1)
                        tt(wsml[:, :, :], wsm[:, :, :], wsmh[:, :, :].bitcast(fp32), ALU.subtract).then_inc(sem("wsm_lo"), 1)
                slots(UB["mem"], 0, 4 * U_D, tasks)

            def small_steps(j):
                if j == 2:
                    ve.wait_ge(sem("tanh_b"), 1)
                    ts(st[:, 2], stw[:, 0], 0.5, 0.5, ALU.mult, ALU.add).then_inc(sem("beta"), 1)
                    tt(stw[:, 1], small[:, :, RANK + GDN_H:32], dtb[:, :].unsqueeze(1).broadcast_to([P, NT, GDN_H]),
                       ALU.add).then_inc(sem("a_bias"), 1)
                if j == 4:
                    ve.wait_ge(sem("softplus"), 1)
                    stt(stw[:, 2], stw[:, 1], 0.0, stw[:, 2], ALU.max, ALU.add).then_inc(sem("softplus_sum"), 1)
                    ve.wait_ge(sem("softplus_sum"), 1)
                    stt(st[:, 0], stw[:, 2], -1.0, alog[:, :].unsqueeze(1).broadcast_to([P, NT, GDN_H]), ALU.mult,
                        ALU.mult).then_inc(sem("logdecay"), 1)
                if j == 8:
                    ve.wait_ge(sem("exp_g"), 1)
                    nc.vector.tensor_copy(st[:, 1].rearrange("p t h -> p (t h)"), mix[:, 2, 0:16]).then_inc(sem("g_out"), 1)
                    ve.wait_ge(sem("g_out"), 1)
                    ve.wait_ge(sem("beta"), 1)
                    tt(stw[:, 0], mix[:, 2, 16:32].rearrange("p (t h) -> p t h", t=NT), st[:, 1], ALU.subtract).then_inc(sem("g_rest"), 1)
                    stt(st[:, 3], st[:, 2], -1.0, stw[:, 3], ALU.mult, ALU.mult).then_inc(sem("neg_beta"), 1)
                    ve.wait_ge(sem("neg_beta"), 1)
                    ve.wait_ge(sem("exp_rest"), 1)

            def mixer_steps(slot, g):
                j = STEP_AT[slot]
                if j is None:
                    return
                need = lambda name, n=None: ve.wait_ge(sem(name), g + 1 if n is None else n)

                def conv_taps(b):
                    need("conv_seed", g * 3 + b + 1)
                    for s in range(1, TAPS):
                        if s > 1:
                            need("conv_tap", g * 6 + 2 * b + s - 1)
                        for h in range(2):
                            y = conv[:, 2 * b + h, s:SEQ]
                            ins = stt(y, mix[:, b, h * SEQ:(h + 1) * SEQ - s], cwg[:, 3 * (TAPS - 1 - s) + b, h:h + 1], y,
                                      ALU.mult, ALU.add)
                        ins.then_inc(sem("conv_tap" if s < TAPS - 1 else "conv_done"), 1)

                if j == 0:
                    groups_done(ve, g)
                    nc.vector.tensor_copy(gs[:, :, :], st[:, :, :, ds(g * 2, 2)].rearrange("p a t h -> p (a t) h")).then_inc(sem("group_consts"), 1)
                    nc.vector.tensor_copy(cwg[:, :, :], convT[:, :, :, ds(g * 2, 2)].rearrange("p a b h -> p (a b) h")).then_inc(sem("group_consts"), 1)
                    nc.vector.tensor_copy(blr[:, :], vecT[:, ds(g + 4 * KT_D, 1)]).then_inc(sem("group_consts"), 1)
                    conv_taps(0)
                if j == 1:
                    need("qexp_ready")
                    need("group_consts", g * 3 + 3)
                    for h in range(2):
                        for t in range(NT):
                            u = 2 * h + t
                            stt(decT[:, u, :], m4(3)[:, u, :], gs[:, 2 + t, h:h + 1], lowA[:, :], ALU.subtract, ALU.min)
                            ins = stt(dec[:, u, :], m4(3)[:, u, :], gs[:, 2 + t, h:h + 1], highB[:, :], ALU.subtract, ALU.max)
                    ins.then_inc(sem("dexp_ready"), 1)
                    conv_taps(1)
                if j == 2:
                    conv_taps(2)
                if j == 4:
                    need("xa_scores")
                    nc.vector.tensor_reduce(mx[:, 0, :], m2(3), AXX, ALU.max).then_inc(sem("xa_max"), 1)
                    need("xa_max")
                    ts(mx[:, 1, :], mx[:, 0, :], -(XA_D ** -0.5), None, ALU.mult).then_inc(sem("xa_nb"), 1)
                if j == 5:
                    need("rn_ready")
                    cv = conv[:, 0:4, :].rearrange("p a b -> p (a b)")
                    tt(cv, cv, rn, ALU.mult)
                    need("ssq_done")
                    for h in range(2):
                        for t in range(NT):
                            u = 2 * h + t
                            ins = ts(vb[:, u, :], m4(2)[:, u, :], gs[:, 4 + t, h:h + 1], None, ALU.mult)
                    ins.then_inc(sem("vb_ready"), 1)
                    need("xa_exp")
                    nc.vector.reciprocal(mx[:, 3, :], mx[:, 2, :]).then_inc(sem("xa_rec"), 1)
                    need("xa_rec")
                    for t in range(NT):
                        ins = ts(prob[:, t, :], prob[:, t, :], mx[:, 3, t:t + 1], None, ALU.mult)
                    ins.then_inc(sem("prob_ready"), 1)
                if j == 6:
                    need("kk_done")
                    need("dec_ready")
                    for h in range(2):
                        for t in range(NT):
                            u = 2 * h + t
                            stt(lmat[:, u, :], m4(2)[:, u, :], gs[:, 4 + t, h:h + 1], dec[:, u, :], ALU.mult, ALU.mult)
                    tt(attnT, m4(0), decT[:, :, :], ALU.mult).then_inc(sem("l_ready"), 1)
                    need("qexp_ready")
                    tt(qe[:, :, :], conv[:, 0:2, P:2 * P], qe[:, :, :], ALU.mult).then_inc(sem("qe_ready"), 1)
                for n in range(4):
                    if j == 13 + 2 * n:
                        need("gla_s", g * 4 + n + 1)
                        if n == 0:
                            need("att_zero")
                        else:
                            need("att_ready", g * 4 + n)
                for l in range(7):
                    mask = lev[:, l, :].unsqueeze(1).broadcast_to([P, 4, P])
                    if j == 7 + 2 * l:
                        need("ux_done", g * 7 + l + 1)
                        tt(zb[:, :, :], m4(0), mask, ALU.mult).then_inc(sem("z_ready"), 1)
                    if j == 8 + 2 * l:
                        need("xz_done", g * 7 + l + 1)
                        eye = ident.unsqueeze(1).broadcast_to([P, 4, P])
                        if l == 0:
                            need("z_ready", g * 7 + 1)
                            tt(xinv, eye, zb[:, :, :], ALU.subtract)
                            tt(tinv, eye, m4(1), ALU.subtract).then_inc(sem("xt_ready"), 1)
                        else:
                            need("xt_ready", g * 7 + l)
                            tt(xinv, xinv, m4(1), ALU.subtract).then_inc(sem("xt_ready"), 1)
                if j == 8:
                    need("xa_hi")
                    tt(o_lo[:, 2, ds(g * 2, 2), :], m2(3), o_hi[:, 2, ds(g * 2, 2), :].bitcast(fp32), ALU.subtract).then_inc(sem("xa_lo"), 1)
                if j == 10:
                    need("lsl", g * 2 + 1)
                    ts(lsn, mix[:, 3, 0:SEQ], blr[:, 0:1], 0.0, ALU.add, ALU.min).then_inc(sem("lsn_ready"), 1)
                if j == 11:
                    need("lsl_ready")
                    need("lsn_ready")
                    for t in range(NT):
                        cols = slice(t * P, (t + 1) * P)
                        ins = nc.vector.tensor_tensor_scan(cb[:, t, :], lsn[:, cols], lsl[:, cols], 0.0, ALU.add, ALU.subtract)
                    ins.then_inc(sem("cb_ready"), 1)
                    need("cb_ready")
                for n in range(4):
                    levels = ((1, 0),) if n == 0 else ((0, 2 * n - 1), (1, 2 * n))
                    if j == 11 + 2 * n:
                        for li, l in levels:
                            m = 1 << l
                            v = cb[:, :, :].rearrange("p t n -> p (t n)").rearrange("p (b m) -> p b m", m=2 * m)
                            ins = tt(ge[:, li, :].rearrange("p (b m) -> p b m", m=2 * m), v,
                                     v[:, :, m - 1:m].broadcast_to([P, SEQ // (2 * m), 2 * m]), ALU.subtract)
                        ins.then_inc(sem("gd_ready"), 1)
                    if j == 13 + 2 * n:
                        nc.vector.copy_predicated(
                            att[:, :, :, :], masks[:, 2 * n:2 * n + 2, :].bitcast(u32).unsqueeze(2).broadcast_to([P, 2, NT, P]),
                            mix[:, 3, :].rearrange("p (l t n) -> p l t n", l=2, t=NT)).then_inc(sem("att_ready"), 1)
                    if j == 12 + 2 * n:
                        need("gexp", g * 4 + n + 1)
                        lo = levels[0][0]
                        qb = gqk[:, 0, :].unsqueeze(1).broadcast_to([P, 2 - lo, SEQ])
                        kb = gqk[:, 1, :].unsqueeze(1).broadcast_to([P, 2 - lo, SEQ])
                        tt(gq[:, lo:2, :], qb, ge[:, lo:2, :], ALU.mult)
                        tt(ge[:, lo:2, :], kb, ge[:, lo:2, :], ALU.mult).then_inc(sem("gqe_ready"), 1)
                if j == 20:
                    need("att_ready", g * 4 + 4)
                    tt(att[:, 0], att[:, 0], att[:, 1], ALU.add).then_inc(sem("att_sum"), 1)
                    need("gxe_ready")
                    tt(gq[:, 0, 0:P], gqk[:, 0, P:2 * P], ge[:, 0, 0:P], ALU.mult)
                    tt(gq[:, 0, P:2 * P], gqk[:, 1, 0:P], ge[:, 0, P:2 * P], ALU.mult).then_inc(sem("gx_ready"), 1)
                vn4 = vnew.rearrange("p (h t) n -> p h t n", t=NT)
                if j == 21:
                    need("gdn_uw")
                    nc.vector.tensor_copy(vn4[:, :, 0, :], m4(0)[:, 0:2, :]).then_inc(sem("vn_ready"), 1)
                if j == 23:
                    need("gdn_v1")
                    nc.vector.tensor_copy(vn4[:, :, 1, :], m4(0)[:, 0:2, :]).then_inc(sem("vn_ready"), 1)
                    need("gsq_ready")
                    nc.vector.tensor_reduce(gss[:, :], gq[:, :, :], AXX, ALU.add).then_inc(sem("gss_ready"), 1)
                if j == 24:
                    need("osq_ready")
                    nc.vector.tensor_reduce(oss[:, :], osq[:, :, :], AXX, ALU.add).then_inc(sem("oss_ready"), 1)
                if j == 25:
                    need("grn_ready")
                    need("rg_ready")
                    for t in range(NT):
                        ins = stt(ggo[:, t, :], m2(3)[:, t, :], gss[:, t:t + 1], rg[:, t, :], ALU.mult, ALU.mult)
                    ins.then_inc(sem("ggo_ready"), 1)
                    need("orn_ready")
                    need("zg_ready")
                    for h in range(2):
                        for t in range(NT):
                            u = 2 * h + t
                            ins = stt(og[:, u, :], m4(2)[:, u, :], oss[:, u:u + 1], zg[:, t, h * P:(h + 1) * P], ALU.mult, ALU.mult)
                    ins.then_inc(sem("og_ready"), 1)
                if j == 26:
                    need("gla_hi")
                    tt(o_lo[:, 0, ds(g * 2, 2), :], m2(3), o_hi[:, 0, ds(g * 2, 2), :].bitcast(fp32), ALU.subtract).then_inc(sem("gla_lo"), 1)
                if j == 27:
                    need("gdn_hi")
                    tt(o_lo[:, 1, ds(g * 2, 2), :], m2(0), o_hi[:, 1, ds(g * 2, 2), :].bitcast(fp32), ALU.subtract).then_inc(sem("gdn_lo"), 1)

            def group(g, mixed):
                slots(UB["proj"], g, 4 * U_D, small_steps if mixed is None else (lambda j: mixer_steps(j, mixed)))

            def gate_logits(p, mixed):
                slots(UB[f"gates{p}"], 0, 6 * U_D, (lambda j: mixer_steps(j, mixed)) if mixed is not None else
                      (lambda j: mixture(2 * p - 1) if j == 1 else None))

            def mixture(n):
                rows = slice(4 * n, 4 * n + 4)
                lower(T_M + n, x_lo[:, rows, :], x_hi[:, rows, :], 0, scale=0.5)

            def up(p):
                def tasks(j):
                    if j % U_O == U_O - 1:
                        k = j // U_O
                        n, br = 2 * p + k // 3, k % 3
                        ve.wait_ge(unit_used, UB[f"up{p}"] + j + 1)
                        ve.wait_ge(sem("gate_ready"), 6 * p + k + 1)
                        if br == 0:
                            ve.wait_ge(t_done, T_M + n)
                            stt(msum[:, :, :], gates[:, k], 1.0, acc[:, k % 2], ALU.add, ALU.mult).then_inc(acc_out[k % 2], 1)
                        else:
                            stt(mtmp[:, :, :], gates[:, k], 1.0, acc[:, k % 2], ALU.add, ALU.mult).then_inc(acc_out[k % 2], 1)
                            ve.wait_ge(acc_out[k % 2], QB[f"up{p}"] // 2 + k // 2 + 1)
                            ve.wait_ge(acc_out[(k - 1) % 2], QB[f"up{p}"] // 2 + (k - 1) // 2 + 1)
                            tt(msum[:, :, :], msum[:, :, :], mtmp[:, :, :], ALU.add).then_inc(sem("m_part" if br == 1 else "m_ready"), 1)
                            ve.wait_ge(sem("m_part" if br == 1 else "m_ready"), n + 1)
                    if j == 13:
                        mixture(2 * p)
                slots(UB[f"up{p}"], 0, 6 * U_O, tasks)

            def output():
                def tasks(j):
                    if j == 1:
                        mixture(3)
                    if j % U_D == U_D - 1:
                        take_product(UB["out"] + j, j // U_D % 2, 1, j // U_D)
                    if j == 4 * U_D - 1:
                        norm_sum(R_OUT)
                        residual(1, R_OUT, 0)
                slots(UB["out"], 0, 4 * U_D, tasks)

            ve.wait_ge(sem("vecT_ready"), 1)
            for s in range(RING):
                if s % 2 == 0:
                    first_lower(0, s // 2)
                ve.wait_ge(hi_ready, s + 1)
                tt(wlo[:, s], raw[:, s], whi[:, s].bitcast(fp32), ALU.subtract).then_inc(lo_ready, 1)
            gu(0, 0, True)
            with ve.Fori(1, N_GU) as i:
                gu(0, i, False)
            down(0)
            memory()
            group(0, None)
            with ve.Fori(1, NG) as g:
                group(g, g - 1)
            gate_logits(0, NG - 1)
            up(0)
            gate_logits(1, None)
            up(1)
            output()
            residual(1, R_OUT, 1)
            first_lower(1, 0)
            residual(1, R_OUT, 2)
            first_lower(1, 1)
            gu(1, 0, True)
            with ve.Fori(1, N_GU) as i:
                gu(1, i, False)
            down(1)
            norm_sum(R_D2)
            for c in range(4):
                residual(2, R_D2, c)


_INS = ["x", "mem", "n_ffn1_pre", "w_ffn1_gu", "w_ffn1_down", "n_ffn1_post", "n_mix_pre", "w_in", "gla_w_lr2",
        "gla_b_lr", "gla_norm", "gdn_conv", "gdn_a_log", "gdn_dt_bias", "gdn_norm", "mem_norm", "w_mem_kv",
        "w_up_gla", "w_up_gdn", "w_up_xa", "w_out", "n_mix_post", "n_ffn2_pre", "w_ffn2_gu", "w_ffn2_down",
        "n_ffn2_post"]


def kernel(**inputs):
    import numpy as _np
    import concourse.bacc as _bacc
    from concourse import mybir as _mybir
    from concourse.bass_utils import run_bass_kernel_spmd as _run

    nc = _bacc.Bacc("TRN2", target_bir_lowering=False, num_devices=1)
    f32 = _mybir.dt.float32
    arrays, aps = {}, {}
    for name in _INS:
        arr = _np.ascontiguousarray(inputs[name])
        arrays[name] = arr
        aps[name] = nc.dram_tensor(name, arr.shape, _mybir.dt.from_np(arr.dtype), kind="ExternalInput").ap()
    out = nc.dram_tensor("out", (1, SEQ, D), f32, kind="ExternalOutput").ap()
    h = nc.dram_tensor("h_scratch", (SEQ, D), f32, kind="Internal").ap()
    mk = nc.dram_tensor("mk_scratch", (XA_W, SEQ), f32, kind="Internal").ap()
    mv = nc.dram_tensor("mv_scratch", (SEQ, XA_W), f32, kind="Internal").ap()
    hybrid_layer(nc, aps, out, h, mk, mv)
    r = _run(nc, [arrays], core_ids=[0])
    return r.results[0]["out"]
```
